# Optimizing a Trainium2 kernel written in Bass

```python
import math
import jax, jax.numpy as jnp
from jax import lax
import numpy as np

D_MODEL = 1024
BATCH = 1
SEQ = 512
DEPTH = 1

CHUNK = 64
MIX_WIDTH = D_MODEL
HG_WIDTH = MIX_WIDTH // 2
CONV_WIDTH = MIX_WIDTH - HG_WIDTH
HG_EXPAND = 128
HG_HEADS = HG_WIDTH // HG_EXPAND
HG_DK = HG_EXPAND
HG_DV = HG_WIDTH // HG_HEADS
CONV_K = 3
N_MEM = 256
XA_HEADS = 4
XA_HEAD_DIM = D_MODEL // XA_HEADS
D_FF = ((8 * D_MODEL // 3 + 255) // 256) * 256
IN_COLS = 4 * HG_WIDTH + 3 * CONV_WIDTH
EPS = 1e-6

kernel_name = "hymba_hgrn2_shortconv_macaron_block"

def rmsnorm(x, g):
    xf = x.astype(jnp.float32)
    y = xf * lax.rsqrt(jnp.mean(xf * xf, axis=-1, keepdims=True) + EPS)
    return (y * g.astype(jnp.float32)).astype(x.dtype)

def swiglu(h, w_gu, w_down):
    gate, up = jnp.split(h @ w_gu, 2, axis=-1)
    return (jax.nn.silu(gate) * up) @ w_down

def hgrn2_chunkwise(q, log_f, k, v):
    B, T, H, DK = q.shape
    DV = v.shape[-1]
    n = T // CHUNK

    def to_chunks(a):
        return a.astype(jnp.float32).reshape(B, n, CHUNK, H, a.shape[-1]).transpose(1, 0, 3, 2, 4)

    qc, lfc, kc, vc = to_chunks(q), to_chunks(log_f), to_chunks(k), to_chunks(v)
    causal = jnp.tril(jnp.ones((CHUNK, CHUNK), dtype=bool))

    def step(S, inp):
        qb, lfb, kb, vb = inp
        b = jnp.cumsum(lfb, axis=2)
        diff = b[:, :, :, None, :] - b[:, :, None, :, :]
        decay = jnp.exp(jnp.where(causal[None, None, :, :, None], diff, -jnp.inf))
        attn = jnp.einsum('bhtk,bhtsk,bhsk->bhts', qb, decay, kb)
        o = attn @ vb + jnp.einsum('bhtk,bhkv->bhtv', qb * jnp.exp(b), S)
        b_last = b[:, :, -1:, :]
        S_new = jnp.exp(b_last[:, :, 0, :])[..., None] * S + jnp.einsum(
            'bhsk,bhsv->bhkv', kb * jnp.exp(b_last - b), vb)
        return S_new, o

    S0 = jnp.zeros((B, H, DK, DV), jnp.float32)
    _, o = lax.scan(step, S0, (qc, lfc, kc, vc))
    return o.transpose(1, 0, 3, 2, 4).reshape(B, T, H, DV)

def causal_dwconv(u, w):
    C = u.shape[-1]
    return lax.conv_general_dilated(
        u, w.astype(u.dtype)[:, None, :], window_strides=(1,), padding=[(CONV_K - 1, 0)],
        dimension_numbers=('NWC', 'WIO', 'NWC'), feature_group_count=C)

def token_mixing(h, w_in, lb, hg_norm, conv_w, conv_norm, w_out):
    B, T, _ = h.shape
    p = h @ w_in
    q, fz, i, g, gb, gc, u = jnp.split(
        p, np.cumsum([HG_WIDTH] * 4 + [CONV_WIDTH] * 2).tolist(), axis=-1)
    lbf = lb.astype(jnp.float32)
    f = lbf + (1.0 - lbf) * jax.nn.sigmoid(fz.astype(jnp.float32))
    log_f = jnp.log(f)
    k = 1.0 - f
    shp = (B, T, HG_HEADS, HG_DK)
    o_hg = hgrn2_chunkwise(jax.nn.silu(q).reshape(shp), log_f.reshape(shp),
                           k.reshape(shp), i.reshape(B, T, HG_HEADS, HG_DV))
    o_hg = rmsnorm(o_hg.astype(h.dtype), hg_norm).reshape(B, T, HG_WIDTH) * jax.nn.silu(g)
    o_cv = rmsnorm(gb * causal_dwconv(gc * u, conv_w), conv_norm)
    return jnp.concatenate([o_hg, o_cv], axis=-1) @ w_out

def cross_attention(h, m, wq, wkv, wo):
    B, T, _ = h.shape
    M = m.shape[1]
    q = (h @ wq).reshape(B, T, XA_HEADS, XA_HEAD_DIM)
    k, v = jnp.split(m @ wkv, 2, axis=-1)
    k = k.reshape(B, M, XA_HEADS, XA_HEAD_DIM)
    v = v.reshape(B, M, XA_HEADS, XA_HEAD_DIM)
    s = jnp.einsum('bthd,bmhd->bhtm', q, k).astype(jnp.float32) * (1.0 / math.sqrt(XA_HEAD_DIM))
    pr = jax.nn.softmax(s, axis=-1).astype(v.dtype)
    o = jnp.einsum('bhtm,bmhd->bthd', pr, v).reshape(B, T, D_MODEL)
    return o @ wo

def setup_inputs(seed: int = 0) -> dict:
    key = jax.random.key(seed)
    ks = iter(jax.random.split(key, 32))

    def nrm(shape, scale):
        return jax.random.normal(next(ks), shape, jnp.float32) * scale

    def gain(shape):
        return 1.0 + nrm(shape, 0.02)

    L = DEPTH
    return {
        "x": nrm((BATCH, SEQ, D_MODEL), 1.0),
        "mem": nrm((BATCH, N_MEM, D_MODEL), 1.0),
        "ffn1_norm": gain((L, D_MODEL)),
        "ffn1_w_gu": nrm((L, D_MODEL, 2 * D_FF), D_MODEL ** -0.5),
        "ffn1_w_down": nrm((L, D_FF, D_MODEL), D_FF ** -0.5),
        "mix_norm": gain((L, D_MODEL)),
        "w_in": nrm((L, D_MODEL, IN_COLS), D_MODEL ** -0.5),
        "lb_logits": nrm((DEPTH + 1, HG_WIDTH), 0.5),
        "hg_norm": gain((L, HG_DV)),
        "conv_w": nrm((L, CONV_K, CONV_WIDTH), CONV_K ** -0.5),
        "conv_norm": gain((L, CONV_WIDTH)),
        "w_out": nrm((L, MIX_WIDTH, D_MODEL), MIX_WIDTH ** -0.5),
        "xa_norm": gain((L, D_MODEL)),
        "mem_norm": gain((L, D_MODEL)),
        "xa_wq": nrm((L, D_MODEL, D_MODEL), D_MODEL ** -0.5),
        "xa_wkv": nrm((L, D_MODEL, 2 * D_MODEL), D_MODEL ** -0.5),
        "xa_wo": nrm((L, D_MODEL, D_MODEL), D_MODEL ** -0.5),
        "ffn2_norm": gain((L, D_MODEL)),
        "ffn2_w_gu": nrm((L, D_MODEL, 2 * D_FF), D_MODEL ** -0.5),
        "ffn2_w_down": nrm((L, D_FF, D_MODEL), D_FF ** -0.5),
        "final_norm": gain((D_MODEL,)),
    }

def reference(x, mem, ffn1_norm, ffn1_w_gu, ffn1_w_down, mix_norm, w_in, lb_logits,
              hg_norm, conv_w, conv_norm, w_out, xa_norm, mem_norm, xa_wq, xa_wkv, xa_wo,
              ffn2_norm, ffn2_w_gu, ffn2_w_down, final_norm):
    lower_bounds = jnp.cumsum(jax.nn.softmax(lb_logits.astype(jnp.float32), axis=0), axis=0)
    for l in range(DEPTH):
        x = x + 0.5 * swiglu(rmsnorm(x, ffn1_norm[l]), ffn1_w_gu[l], ffn1_w_down[l])
        x = x + token_mixing(rmsnorm(x, mix_norm[l]), w_in[l], lower_bounds[l],
                             hg_norm[l], conv_w[l], conv_norm[l], w_out[l])
        x = x + cross_attention(rmsnorm(x, xa_norm[l]), rmsnorm(mem, mem_norm[l]),
                                xa_wq[l], xa_wkv[l], xa_wo[l])
        x = x + 0.5 * swiglu(rmsnorm(x, ffn2_norm[l]), ffn2_w_gu[l], ffn2_w_down[l])
    return rmsnorm(x, final_norm)


_drawn_inputs = setup_inputs


def setup_inputs(seed=0):
    import zlib

    import numpy as np

    out = dict(_drawn_inputs(seed))
    spreads = {}
    factors = {'ffn1_norm': 5.079,
     'lb_logits': 3.118,
     'hg_norm': 8.0,
     'conv_norm': 4.782,
     'xa_norm': 8.0,
     'mem_norm': 8.0,
     'ffn2_norm': 8.0,
     'final_norm': 2.952}
    for name, (base, spread) in spreads.items():
        noise = np.random.default_rng([zlib.crc32(name.encode()), seed]).standard_normal(out[name].shape)
        drawn = base * np.exp(spread * noise) if base else spread * noise
        out[name] = __import__('jax').numpy.asarray(drawn.astype(out[name].dtype))
    for name, factor in factors.items():
        out[name] = (out[name] * factor).astype(out[name].dtype)
    return out
```

```python
import concourse.bass as bass
from concourse import mybir
from contextlib import ExitStack

D = 1024
T = 512
KC = D // 128
FF = 2816
FC = FF // 128
HEADS = 4
CC = 4
M = 256
XH = 4
CHUNK = 64
NCH = T // CHUNK
TT = T // 128
EPS = 1e-6
SLOTS = 4
UNIT = 1024
DOWN_SPLIT = [8, 8, 6]
LEVELS = [32, 16, 8, 4, 2, 1]
NL = len(LEVELS) + 1

U_FFN1 = 0
N_UP = 2 * FC
N_DOWN = KC * len(DOWN_SPLIT)
U_DOWN1 = U_FFN1 + N_UP
U_MIX = U_DOWN1 + N_DOWN
U_V = U_MIX
MIX_GROUPS = [("q", 0), ("f", 0), ("g", 0), ("B", 0), ("C", 0), ("u", 0), ("q", 1), ("f", 1), ("g", 1),
              ("B", 1), ("C", 1), ("u", 1), ("q", 2), ("f", 2), ("g", 2), ("q", 3), ("f", 3), ("g", 3),
              ("B", 2), ("C", 2), ("u", 2), ("B", 3), ("C", 3), ("u", 3)]
U_MG = U_V + 4
U_WOUT = U_MG + len(MIX_GROUPS)
U_KT = U_WOUT + KC
U_VX = U_KT + KC
U_WQ = U_VX + 8
U_WO = U_WQ + KC
U_FFN2 = U_WO + KC
U_DOWN2 = U_FFN2 + N_UP
NU = U_DOWN2 + N_DOWN

PARAMS = {}
_at = 0
for _n, _w in (("ffn1", KC), ("mix", KC), ("xa", KC), ("ffn2", KC), ("final", KC), ("mem", KC),
               ("hgn", 1), ("convn", CC), ("convw", 3 * CC), ("lb", 2 * HEADS)):
    PARAMS[_n] = _at
    _at += _w
NPAR = _at

PIECES = {}


def _plan():
    per_head = [("A", 0), ("L", 0), ("L", 1), ("L", 2), ("L", 3), ("L", 4), ("L", 5), ("L", 6),
                ("E", 0), ("U", 0), ("O", 0), ("N", 0)]
    todo = [(k, h, a) for h in range(HEADS) for k, a in per_head]
    ready = {0: 2, 1: 8, 2: 14, 3: 17}
    pos = 2
    while todo:
        n = 0
        while todo and n < 2 and pos >= ready[todo[0][1]]:
            PIECES.setdefault(min(pos, len(MIX_GROUPS) - 1), []).append(todo.pop(0))
            n += 1
        pos += 1


_plan()
CONV_NORM_AT = len(MIX_GROUPS) - 1


def block_kernel(nc, w_all, x_t, mem_t, params, consts_mask, ident_d, out):
    f32 = mybir.dt.float32
    f32r = mybir.dt.float32r
    u8 = mybir.dt.uint8
    ALU = mybir.AluOpType
    ACT = mybir.ActivationFunctionType
    AX = mybir.AxisListType
    MULT, ADD, SUB = ALU.mult, ALU.add, ALU.subtract

    ctx = ExitStack()
    with ctx:
        def sb(name, shape, dt=f32, where=ctx):
            return where.enter_context(nc.sbuf_tensor(name, shape, dt))

        def sem(name):
            return ctx.enter_context(nc.semaphore(name))

        raw = sb("raw", [128, SLOTS, UNIT])
        wh = sb("wh", [128, SLOTS, UNIT], f32r)
        wl = sb("wl", [128, SLOTS, UNIT], f32r)
        x = sb("x", [128, KC, T])
        xh = sb("xh", [128, KC, T], f32r)
        xl = sb("xl", [128, KC, T], f32r)
        rstd = sb("rstd", [128, T])
        acc = sb("acc", [128, T])
        sq = sb("sq", [128, 2, T])
        gbuf = sb("gbuf", [128, 2, T])
        ubuf = sb("ubuf", [128, 2, T])
        convV, lf = ubuf[:, 0, :], ubuf[:, 1, :]
        ones = sb("ones", [128, 128])
        ident = sb("ident", [128, 128])
        masks = sb("masks", [128, NL, 128], u8)
        par = sb("par", [128, NPAR])
        lbs = sb("lbs", [128, 8, HEADS])
        eps = sb("eps", [128, 1])
        cols = sb("cols", [128, 2, TT])

        ffn_mem = ExitStack()
        hid_h = sb("hid_h", [128, FC * T], f32r, ffn_mem)
        hid_l = sb("hid_l", [128, FC * T], f32r, ffn_mem)
        ffn_mem.close()
        cat_h = sb("cat_h", [128, KC, T], f32r)
        cat_l = sb("cat_l", [128, KC, T], f32r)
        mix_mem = ExitStack()
        qb = sb("qb", [128, 2, T], f32, mix_mem)
        fb = sb("fb", [128, 2, T], f32, mix_mem)
        gb = sb("gb", [128, 2, T], f32, mix_mem)
        V = sb("V", [128, TT, 512], f32, mix_mem)
        b = sb("b", [128, T], f32, mix_mem)
        restart = sb("restart", [128, T], f32, mix_mem)
        X = sb("X", [128, 2, T], f32, mix_mem)
        attn = sb("attn", [128, TT, 128], f32, mix_mem)
        eb = sb("eb", [128, T], f32, mix_mem)
        kd = sb("kd", [128, T], f32, mix_mem)
        kdT = sb("kdT", [128, TT, 128], f32, mix_mem)
        S = sb("S", [128, NCH - 1, 128], f32, mix_mem)
        osq = sb("osq", [128, T], f32, mix_mem)
        onrm = sb("onrm", [128, T], f32, mix_mem)
        convB = sb("convB", [128, T], f32, mix_mem)
        convC = sb("convC", [128, T], f32, mix_mem)
        convU = sb("convU", [128, 2 + T], f32, mix_mem)
        convO = sb("convO", [128, CC, T], f32, mix_mem)
        mix_mem.close()
        xa_mem = ExitStack()
        kv_mem = ExitStack()
        memf = sb("memf", [128, KC, M], f32, kv_mem)
        mh = sb("mh", [128, KC, M], f32r, kv_mem)
        ml = sb("ml", [128, KC, M], f32r, kv_mem)
        kv_mem.close()
        qh = sb("qh", [128, 2, 2, T], f32r, xa_mem)
        ql = sb("ql", [128, 2, 2, T], f32r, xa_mem)
        pTh = sb("pTh", [128, 2, T], f32r, xa_mem)
        pTl = sb("pTl", [128, 2, T], f32r, xa_mem)
        kTh = sb("kTh", [128, KC, M], f32r, xa_mem)
        kTl = sb("kTl", [128, KC, M], f32r, xa_mem)
        vxh = sb("vxh", [128, 2, D], f32r, xa_mem)
        vxl = sb("vxl", [128, 2, D], f32r, xa_mem)
        P = sb("P", [128, TT, M], f32, xa_mem)
        smax = sb("smax", [128, TT], f32, xa_mem)
        ssum = sb("ssum", [128, TT], f32, xa_mem)
        xa_mem.close()

        bank = [ctx.enter_context(nc.psum_tensor(f"bank{i}", [128, 512], f32)) for i in range(4)]
        score_bank = [ctx.enter_context(nc.psum_tensor(f"score{i}", [128, 512], f32)) for i in range(2)]
        o_bank = ctx.enter_context(nc.psum_tensor("o_bank", [128, 512], f32))
        n_bank = ctx.enter_context(nc.psum_tensor("n_bank", [128, 512], f32))

        raw_loaded = [sem(f"raw_loaded{i}") for i in range(SLOTS)]
        x_loaded = [sem(f"x_loaded{i}") for i in range(KC)]
        par_loaded = sem("par_loaded")
        mask_loaded = sem("mask_loaded")
        ident_loaded = sem("ident_loaded")
        mem_loaded = sem("mem_loaded")
        out_stored = sem("out_stored")
        hi_ready = sem("hi_ready")
        lo_ready = sem("lo_ready")
        unit_used = sem("unit_used")
        group_read = sem("group_read")
        x_hi = sem("x_hi")
        x_lo = sem("x_lo")
        sq_ready = sem("sq_ready")
        sq_added = sem("sq_added")
        acc_clear = sem("acc_clear")
        n_done = sem("n_done")
        rms_ready = sem("rms_ready")
        silu_ready = sem("silu_ready")
        hid_new = sem("hid_new")
        hid_hi = sem("hid_hi")
        hid_lo = sem("hid_lo")
        dve_step = sem("dve_step")
        consts_ready = sem("consts_ready")
        lb_diff = sem("lb_diff")
        lb_exp = sem("lb_exp")
        act_out = sem("act_out")
        f_ready = sem("f_ready")
        lf_ready = sem("lf_ready")
        diff_ready = sem("diff_ready")
        exp_ready = sem("exp_ready")
        score_in = sem("score_in")
        score_done = sem("score_done")
        score_read = sem("score_read")
        kd_ready = sem("kd_ready")
        kdT_ready = sem("kdT_ready")
        S_ready = sem("S_ready")
        o_done = sem("o_done")
        o_read = sem("o_read")
        osq_ready = sem("osq_ready")
        cat_new = sem("cat_new")
        cat_hi = sem("cat_hi")
        cat_lo = sem("cat_lo")
        conv_new = sem("conv_new")
        mem_norm = sem("mem_norm")
        mem_hi = sem("mem_hi")
        mem_lo = sem("mem_lo")
        kv_hi = sem("kv_hi")
        q_hi = sem("q_hi")
        q_lo = sem("q_lo")
        xs_done = sem("xs_done")
        xmax_ready = sem("xmax_ready")
        p_exp = sem("p_exp")
        p_ready = sem("p_ready")
        att_done = sem("att_done")
        pt_hi = sem("pt_hi")
        pt_lo = sem("pt_lo")

        gain = {n: PARAMS[n] for n in ("ffn1", "mix", "xa", "ffn2", "final", "mem")}

        def pcol(name, i):
            return par[:, PARAMS[name] + i:PARAMS[name] + i + 1]

        G_UP1 = 0
        G_DOWN1 = G_UP1 + N_UP
        G_V = G_DOWN1 + KC
        G_MG = G_V + 4
        G_WOUT = G_MG + len(MIX_GROUPS)
        G_KT = G_WOUT + KC
        G_VX = G_KT + KC
        G_XA = G_VX + 4
        XA_ORDER = [("q", 0), ("q", 1), ("S", 0), ("q", 2), ("q", 3), ("T", 0), ("S", 1), ("O", 0), ("q", 4), ("q", 5),
                    ("T", 1), ("S", 2), ("O", 1), ("q", 6), ("q", 7), ("T", 2), ("S", 3), ("O", 2), ("T", 3), ("O", 3)]
        XG, g = {}, G_XA
        for kind, i in XA_ORDER:
            if kind == "q":
                XG[kind, i] = g
                g += 1
            if kind == "O":
                XG[kind, i] = g
                g += 2
        G_WO = g
        G_UP2 = G_WO + KC
        G_DOWN2 = G_UP2 + N_UP
        X_GROUP = [None, G_DOWN1, G_WOUT, G_WO, G_DOWN2]
        Q_X0, Q_X1, Q_CONV, Q_MEM, Q_X2, Q_X3, Q_X4 = 0, 8, 16, 20, 28, 36, 44
        n_uses = ["ffn1", "mixcol", "mix"]
        for at in range(len(MIX_GROUPS)):
            for kind, h, a in PIECES.get(at, []):
                if kind == "E":
                    n_uses.append(("T", h))
                if kind == "U":
                    n_uses.append(("U", h))
                if kind == "N":
                    n_uses.append(("N", h))
        n_uses += ["conv", "mem", "xa"]
        n_uses += [("pt", i) for i in range(XH)]
        n_uses += ["ffn2", "final"]
        N = {n: i for i, n in enumerate(n_uses)}
        NORMS = ["ffn1", "mix", "conv", "mem", "xa", "ffn2", "final"]
        roots = ["ffn1", "mixcol", "mix"] + [n for n in n_uses if n[0] == "N"] + ["conv", "mem", "xa", "ffn2", "final"]
        R = {n: i for i, n in enumerate(roots)}
        FN = {g: i for i, g in enumerate([g for g in MIX_GROUPS if g[0] in "qfg"])}

        def score_no(h, a):
            return NL * h + a

        def hgrn_cat(h):
            return h

        block = ctx.enter_context(nc.Block())

        @block.sync
        def _(sp):
            for u in range(SLOTS):
                sp.dma_start(raw[:, u, :], w_all[u, :, :]).then_inc(raw_loaded[u], 16)
                if u == 0:
                    sp.dma_start(par[:, :], params).then_inc(par_loaded, 16)
            with sp.Fori(1, NU // SLOTS) as i:
                for c in range(SLOTS):
                    sp.wait_ge(lo_ready, i * SLOTS + (c - SLOTS + 1))
                    sp.dma_start(raw[:, c, :], w_all[bass.ds(i * SLOTS + c, 1), :, :].rearrange("a p n -> p (a n)"))\
                      .then_inc(raw_loaded[c], 16)
            for m in range(KC):
                sp.wait_ge(cat_new, KC + m + 1)
                sp.dma_start(out[m, :, :], x[:, m, :]).then_inc(out_stored, 16)
            sp.wait_ge(out_stored, 16 * KC)

        @block.gpsimd
        def _(pool):
            with pool.Fori(0, NU // SLOTS) as i:
                for c in range(SLOTS):
                    pool.wait_ge(hi_ready, i * SLOTS + (c + 1))
                    nc.gpsimd.tensor_tensor(wl[:, c, :], raw[:, c, :], wh[:, c, :].bitcast(f32), SUB)\
                        .then_inc(lo_ready, 1)

        @block.scalar
        def _(act):
            def hi(u, slot=None, use=None):
                slot = u % SLOTS if slot is None else slot
                use = u // SLOTS if use is None else use
                act.wait_ge(raw_loaded[slot], (use + 1) * 16)
                if not (isinstance(u, int) and u < SLOTS):
                    act.wait_ge(unit_used, u + (1 - SLOTS))
                nc.scalar.activation(wh[:, slot, :], raw[:, slot, :], ACT.Copy).then_inc(hi_ready, 1)

            def ahead(u, i=None, base=0):
                if i is None:
                    if u + SLOTS < NU:
                        hi(u + SLOTS)
                else:
                    hi(i + (u + SLOTS), (u + SLOTS) % SLOTS, None)

            def ahead_loop(first, i4, c):
                u = first + c + SLOTS
                slot = u % SLOTS
                act.wait_ge(raw_loaded[slot], i4 * (16 // SLOTS) + 16 * (u // SLOTS + 1))
                act.wait_ge(unit_used, i4 + (u + 1 - SLOTS))
                nc.scalar.activation(wh[:, slot, :], raw[:, slot, :], ACT.Copy).then_inc(hi_ready, 1)

            def square(src, n, width=T):
                if n >= 2 if isinstance(n, int) else True:
                    act.wait_ge(sq_added, n - 1)
                slot = n % 2
                nc.scalar.activation(sq[:, slot, 0:width], src, ACT.Square).then_inc(sq_ready, 1)

            def new_x(phase, m, qn, split=True, i=None):
                off = 0 if i is None else i * 4
                chunk = m if i is None else None
                xs = x[:, m, :] if i is None else x[:, bass.ds(i * 4 + m, 1), :].rearrange("p a t -> p (a t)")
                if i is not None:
                    pass
                elif phase > 0:
                    act.wait_ge(group_read, X_GROUP[phase] + m + 5)
                else:
                    act.wait_ge(x_loaded[m], 16)
                if split:
                    name = ["ffn1", "mix", "xa", "ffn2"][phase]
                    if i is None:
                        dst, gcol = xh[:, m, :], pcol(name, m)
                    else:
                        dst = xh[:, bass.ds(i * 4 + m, 1), :].rearrange("p a t -> p (a t)")
                        gcol = par[:, bass.ds(i * 4 + (gain[name] + m), 1)]
                    nc.scalar.activation(dst, xs, ACT.Copy, scale=gcol).then_inc(x_hi, 1)
                if i is None and qn + m >= 2:
                    act.wait_ge(sq_added, qn + m - 1)
                nc.scalar.activation(sq[:, (qn + m) % 2, :], xs, ACT.Square).then_inc(sq_ready, 1)

            def root(name, dst, src, width):
                act.wait_ge(n_done, N[name] + 1)
                nc.scalar.activation(dst, src, ACT.Sqrt, bias=eps[:, :], scale=1.0 / width).then_inc(rms_ready, 1)

            def root_of(name, width=D, cols_=T):
                act.wait_ge(n_done, N[name] + 1)
                nc.scalar.activation(rstd[:, 0:cols_], n_bank[:, 0:cols_], ACT.Sqrt, bias=eps[:, :],
                                           scale=1.0 / width)\
                    .then_inc(rms_ready, 1)

            def ffn(first, last, norm, which):
                u0, g0, hb = (U_FFN1, G_UP1, 0) if which == 0 else (U_FFN2, G_UP2, FC)

                def up(i, j):
                    ahead_loop(u0, i * 4, 2 * j)
                    act.wait_ge(group_read, i * 4 + (g0 + 2 * j + 5))
                    nc.scalar.activation(gbuf[:, j, :], gbuf[:, j, :], ACT.Silu).then_inc(silu_ready, 1)
                    act.wait_ge(hid_new, i * 2 + (hb + j + 1))
                    ahead_loop(u0, i * 4, 2 * j + 1)
                    nc.scalar.activation(hid_h[:, bass.ds(i * (2 * T) + j * T, T)], ubuf[:, j, :], ACT.Copy)\
                        .then_inc(hid_hi, 1)

                act_first = True
                for j in range(2):
                    if j == 0:
                        ahead(u0)
                        root_of(norm)
                        act.wait_ge(group_read, g0 + 2 * j + 5)
                        nc.scalar.activation(gbuf[:, j, :], gbuf[:, j, :], ACT.Silu).then_inc(silu_ready, 1)
                        ahead(u0 + 1)
                    else:
                        ahead(u0 + 2)
                        act.wait_ge(group_read, g0 + 2 * j + 5)
                        nc.scalar.activation(gbuf[:, j, :], gbuf[:, j, :], ACT.Silu).then_inc(silu_ready, 1)
                        ahead(u0 + 3)
                    act.wait_ge(hid_new, hb + j + 1)
                    nc.scalar.activation(hid_h[:, j * T:(j + 1) * T], ubuf[:, j, :], ACT.Copy).then_inc(hid_hi, 1)
                with act.Fori(1, FC // 2) as i:
                    up(i, 0)
                    up(i, 1)
                ud = u0 + N_UP
                nd = len(DOWN_SPLIT)
                phase = 1 if which == 0 else 4
                qn = Q_X1 if which == 0 else Q_X4
                if which == 0:
                    with act.Fori(0, KC // 4) as i:
                        for m in range(4):
                            for c in range(nd):
                                if c == nd - 1:
                                    act.wait_ge(group_read, i * 4 + (X_GROUP[phase] + m + 5))
                                    act.wait_ge(sq_added, i * 4 + (qn + m - 1))
                                ahead_loop(ud, i * (4 * nd), m * nd + c)
                            new_x(phase, m, qn, True, i)
                else:
                    for m in range(KC):
                        for c in range(nd):
                            ahead(ud + m * nd + c)
                        new_x(phase, m, qn, False)

            act.dma_start(x[:, 0, :], x_t[0, :, :]).then_inc(x_loaded[0], 16)
            for m in range(1, KC):
                act.dma_start(x[:, m, :], x_t[m, :, :]).then_inc(x_loaded[m], 16)
            act.dma_start(ident[:, :], ident_d).then_inc(ident_loaded, 16)
            act.dma_start(gbuf[:, :, :].rearrange("p a t -> p (a t)")[:, 0:NL * 128], consts_mask)\
               .then_inc(mask_loaded, 16)
            act.wait_ge(par_loaded, 16)
            hi(0)
            for m in range(KC):
                new_x(0, m, Q_X0)
                if m < 3:
                    hi(m + 1)
            act.wait_ge(lb_diff, 1)
            nc.scalar.activation(lbs[:, 1:3, :], lbs[:, 1:3, :], ACT.Exp).then_inc(lb_exp, 1)
            ffn(0, 0, "ffn1", 0)

            for k in range(4):
                ahead(U_V + k)
                if k == 0:
                    act.wait_ge(n_done, N["mixcol"] + 1)
                    nc.scalar.activation(cols[:, 0, :], n_bank[:, 0:TT], ACT.Sqrt, bias=eps[:, :],
                                               scale=1.0 / D)\
                        .then_inc(rms_ready, 1)
                    root_of("mix")

            def piece(kind, h, a):
                if kind == "A":
                    act.wait_ge(f_ready, h + 1)
                    nc.scalar.activation(lf, fb[:, h % 2, :], ACT.Ln).then_inc(lf_ready, 1)
                if kind == "L" and a < len(LEVELS):
                    act.wait_ge(diff_ready, len(LEVELS) * h + a + 1 + h)
                    nc.scalar.activation(X[:, a % 2, :], X[:, a % 2, :], ACT.Exp).then_inc(exp_ready, 1)
                if kind == "E":
                    act.wait_ge(diff_ready, (len(LEVELS) + 1) * (h + 1))
                    nc.scalar.activation(eb[:, :], b[:, :], ACT.Exp)
                    nc.scalar.activation(kd[:, :], kd[:, :], ACT.Exp).then_inc(exp_ready, 1)
                if kind == "O":
                    act.wait_ge(o_done, h + 1)
                    nc.scalar.activation(osq[:, :], o_bank[:, :], ACT.Square).then_inc(osq_ready, 1)
                if kind == "N":
                    act.wait_ge(n_done, N["N", h] + 1)
                    nc.scalar.activation(osq[:, :], n_bank[:, :], ACT.Sqrt, bias=eps[:, :], scale=1.0 / 128)\
                        .then_inc(rms_ready, 1)
                    act.wait_ge(cat_new, h + 1)
                    nc.scalar.activation(cat_h[:, h, :], onrm[:, :], ACT.Copy).then_inc(cat_hi, 1)

            for at, (kind, c) in enumerate(MIX_GROUPS):
                ahead(U_MG + at)
                if kind in "qfg":
                    buf = {"q": qb, "f": fb, "g": gb}[kind]
                    act.wait_ge(group_read, G_MG + at + 5)
                    nc.scalar.activation(buf[:, c % 2, :], buf[:, c % 2, :],
                                         ACT.Sigmoid if kind == "f" else ACT.Silu).then_inc(act_out, 1)
                if kind == "u":
                    act.wait_ge(conv_new, c + 1)
                    square(convO[:, c, :], Q_CONV + c)
                for p in PIECES.get(at, []):
                    piece(*p)
            act.wait_ge(n_done, N["conv"] + 1)
            nc.scalar.activation(osq[:, :], n_bank[:, :], ACT.Sqrt, bias=eps[:, :], scale=1.0 / 512)\
                .then_inc(rms_ready, 1)
            for c in range(CC):
                act.wait_ge(cat_new, HEADS + c + 1)
                nc.scalar.activation(cat_h[:, HEADS + c, :], convO[:, c, :], ACT.Copy).then_inc(cat_hi, 1)
            act.wait_ge(cat_lo, KC)
            act.dma_start(memf[:, :, :], mem_t).then_inc(mem_loaded, 16)
            ahead(U_WOUT)
            act.wait_ge(mem_loaded, 16)
            for k in range(KC):
                square(memf[:, k, :], Q_MEM + k, M)
            ahead(U_WOUT + 1)
            act.wait_ge(n_done, N["mem"] + 1)
            nc.scalar.activation(rstd[:, 0:M], n_bank[:, 0:M], ACT.Sqrt, bias=eps[:, :], scale=1.0 / D)\
                .then_inc(rms_ready, 1)
            for k in range(KC):
                act.wait_ge(mem_norm, k + 1)
                nc.scalar.activation(mh[:, k, :], memf[:, k, :], ACT.Copy).then_inc(mem_hi, 1)
            for m in range(KC):
                if m >= 2:
                    ahead(U_WOUT + m)
                new_x(2, m, Q_X2)
            for g in range(KC):
                ahead(U_KT + g)
                if g == 0:
                    root_of("xa")
                act.wait_ge(unit_used, U_KT + g + 1)
                nc.scalar.activation(kTh[:, g, :], bank[(G_KT + g) % 4][:, 0:M], ACT.Copy).then_inc(kv_hi, 1)
            for half in range(2):
                for c in range(4):
                    ahead(U_VX + 4 * half + c)
                for t in range(2):
                    g = G_VX + 2 * half + t
                    act.wait_ge(unit_used, U_VX + 4 * half + 4)
                    nc.scalar.activation(vxh[:, t, 512 * half:512 * half + 512], bank[g % 4][:, :], ACT.Copy)\
                        .then_inc(kv_hi, 1)
            for kind, i in XA_ORDER:
                if kind == "q":
                    ahead(U_WQ + i)
                    act.wait_ge(group_read, XG["q", i] + 5)
                    nc.scalar.activation(qh[:, (i // 2) % 2, i % 2, :], gbuf[:, i % 2, :], ACT.Copy)\
                        .then_inc(q_hi, 1)
                if kind == "S":
                    for t in range(TT):
                        act.wait_ge(xmax_ready, i + 1)
                        nc.scalar.activation(P[:, t, :], score_bank[t // 2][:, (t % 2) * M:(t % 2 + 1) * M], ACT.Exp,
                                             bias=smax[:, t:t + 1], scale=1.0 / 16, accum_out=ssum[:, t:t + 1])\
                            .then_inc(p_exp, 1)
                if kind == "T":
                    for t, bk in enumerate((o_bank, n_bank)):
                        act.wait_ge(n_done, N["pt", i] + 1)
                        nc.scalar.activation(pTh[:, t, :], bk[:, :], ACT.Copy).then_inc(pt_hi, 1)
                if kind == "O":
                    for d in range(2):
                        g = XG["O", i] + d
                        act.wait_ge(att_done, 2 * i + d + 1)
                        nc.scalar.activation(cat_h[:, 2 * i + d, :], bank[g % 4][:, :], ACT.Copy).then_inc(cat_hi, 1)
            for m in range(KC):
                ahead(U_WO + m)
                new_x(3, m, Q_X3)
            ffn(0, 0, "ffn2", 1)
            root_of("final")

        @block.vector
        def _(dve):
            steps = [0]

            def link(ins):
                steps[0] += 1
                ins.then_inc(dve_step, 1)
                dve.wait_ge(dve_step, steps[0])
                return ins

            V_ = nc.vector
            V_.memset(ones[:, :], 1.0).then_inc(consts_ready, 1)
            V_.memset(eps[:, :], EPS).then_inc(consts_ready, 1)
            link(V_.memset(acc[:, :], 0.0))
            V_.memset(rstd[:, :], 0.0).then_inc(group_read, 4)

            dve.wait_ge(par_loaded, 16)
            l0 = par[:, PARAMS["lb"]:PARAMS["lb"] + HEADS]
            l1 = par[:, PARAMS["lb"] + HEADS:PARAMS["lb"] + 2 * HEADS]
            link(V_.tensor_tensor(lbs[:, 0, :], l0, l1, ALU.max))
            V_.tensor_tensor(lbs[:, 1, :], l0, lbs[:, 0, :], SUB)
            V_.tensor_tensor(lbs[:, 2, :], l1, lbs[:, 0, :], SUB).then_inc(lb_diff, 1)

            def chunk_lo(phase, m, qn, i=None, split=True):
                off = 0 if i is None else i * 4
                if split:
                    name = ["ffn1", "mix", "xa", "ffn2"][phase]
                    if i is None:
                        xs, dh, dl, gcol = x[:, m, :], xh[:, m, :], xl[:, m, :], pcol(name, m)
                    else:
                        xs, dh, dl = (t[:, bass.ds(i * 4 + m, 1), :].rearrange("p a t -> p (a t)") for t in (x, xh, xl))
                        gcol = par[:, bass.ds(i * 4 + (gain[name] + m), 1)]
                    dve.wait_ge(x_hi, off + (KC * phase + m + 1))
                    V_.scalar_tensor_tensor(out=dl, in0=xs, scalar=gcol, in1=dh.bitcast(f32), op0=MULT, op1=SUB)\
                        .then_inc(x_lo, 1)
                add_squares(qn + m, off)

            def add_squares(n, off=0, width=T):
                dve.wait_ge(sq_ready, off + (n + 1))
                if n > 0:
                    dve.wait_ge(sq_added, off + n)
                V_.tensor_tensor(acc[:, 0:width], acc[:, 0:width], sq[:, n % 2, 0:width], ADD).then_inc(sq_added, 1)

            def clear_acc():
                V_.memset(acc[:, :], 0.0).then_inc(acc_clear, 1)
                link(V_.memset(eps[:, :], EPS)) if False else None

            def inverse(name, dst):
                dve.wait_ge(rms_ready, R[name] + 1)
                link(V_.reciprocal(dst, dst))

            def norm_of(name):
                inverse(name, rstd[:, :])
                clear()

            cleared = [0]

            def clear():
                cleared[0] += 1
                V_.memset(acc[:, :], 0.0).then_inc(acc_clear, 1)
                dve.wait_ge(acc_clear, cleared[0])

            def update_x(m, g, u, scale, i=None, nd=1):
                off = 0 if i is None else i * 4
                xs = x[:, m, :] if i is None else x[:, bass.ds(i * 4 + m, 1), :].rearrange("p a t -> p (a t)")
                dve.wait_ge(unit_used, (0 if i is None else i * (4 * nd)) + (u + nd * (m + 1)))
                V_.scalar_tensor_tensor(out=xs, in0=bank[(g + m) % 4][:, :], scalar=scale, in1=xs,
                                        op0=MULT, op1=ADD).then_inc(group_read, 1)

            def ffn(norm, which):
                u0, g0, hb = (U_FFN1, G_UP1, 0) if which == 0 else (U_FFN2, G_UP2, FC)

                def up(i, j, first=False):
                    gi = 0 if first else i * 4
                    ji = 0 if first else i * 2
                    ga, gu = g0 + 2 * j, g0 + 2 * j + 1
                    dve.wait_ge(unit_used, gi + (u0 + 2 * j + 1))
                    V_.tensor_tensor(gbuf[:, j, :], bank[ga % 4][:, :], rstd[:, :], MULT).then_inc(group_read, 1)
                    dve.wait_ge(unit_used, gi + (u0 + 2 * j + 2))
                    V_.tensor_tensor(ubuf[:, j, :], bank[gu % 4][:, :], rstd[:, :], MULT).then_inc(group_read, 1)
                    dve.wait_ge(group_read, gi + (gu + 1 + 4))
                    dve.wait_ge(silu_ready, ji + (hb + j + 1))
                    V_.tensor_tensor(ubuf[:, j, :], ubuf[:, j, :], gbuf[:, j, :], MULT).then_inc(hid_new, 1)
                    dve.wait_ge(hid_hi, ji + (hb + j + 1))
                    hs = slice(j * T, (j + 1) * T) if first else bass.ds(i * (2 * T) + j * T, T)
                    V_.tensor_tensor(hid_l[:, hs], ubuf[:, j, :], hid_h[:, hs].bitcast(f32), SUB).then_inc(hid_lo, 1)

                norm_of(norm)
                up(0, 0, True)
                up(0, 1, True)
                with dve.Fori(1, FC // 2) as i:
                    up(i, 0)
                    up(i, 1)
                gd = g0 + N_UP
                if which == 0:
                    with dve.Fori(0, KC // 4) as i:
                        for m in range(4):
                            update_x(m, gd, U_DOWN1, 0.5, i, len(DOWN_SPLIT))
                            chunk_lo(1, m, Q_X1, i)
                else:
                    for m in range(KC):
                        update_x(m, gd, U_DOWN2, 0.5, None, len(DOWN_SPLIT))
                        chunk_lo(4, m, Q_X4, None, False)

            for m in range(KC):
                chunk_lo(0, m, Q_X0)
            dve.wait_ge(lb_exp, 1)
            link(V_.tensor_tensor(lbs[:, 3, :], lbs[:, 1, :], lbs[:, 2, :], ADD))
            link(V_.reciprocal(lbs[:, 4, :], lbs[:, 3, :]))
            link(V_.tensor_tensor(lbs[:, 5, :], lbs[:, 1, :], lbs[:, 4, :], MULT))
            link(V_.tensor_scalar(lbs[:, 6, :], lbs[:, 5, :], -1.0, 1.0, MULT, ADD))
            dve.wait_ge(mask_loaded, 16)
            link(V_.tensor_copy(masks[:, :, :].rearrange("p l s -> p (l s)"),
                                gbuf[:, :, :].rearrange("p a t -> p (a t)")[:, 0:NL * 128]))
            ffn("ffn1", 0)

            V_.memset(restart[:, :], 1.0).then_inc(dve_step, 1)
            steps[0] += 1
            dve.wait_ge(dve_step, steps[0])
            V_.memset(restart[:, :].rearrange("p (c t) -> p c t", t=CHUNK)[:, :, 0:1], 0.0)
            V_.memset(attn[:, :, :], 0.0)
            link(V_.memset(convU[:, 0:2], 0.0))
            dve.wait_ge(rms_ready, R["mixcol"] + 1)
            link(V_.reciprocal(cols[:, 1, :], cols[:, 0, :]))
            norm_of("mix")
            for t in range(TT):
                g = G_V + t
                dve.wait_ge(unit_used, U_V + 4)
                V_.tensor_scalar(V[:, t, :], bank[g % 4][:, :], cols[:, 1, t:t + 1], None, MULT)\
                    .then_inc(group_read, 1)

            def blocks(t_, m):
                return t_.rearrange("p (n s m) -> p n s m", s=2, m=m)

            def differences(h, a):
                m = LEVELS[a]
                nb = T // (2 * m)
                if h or a >= 2:
                    dve.wait_ge(score_done, score_no(h, a - 2) + 1 if a >= 2 else score_no(h - 1, a + 4) + 1)
                bb, xx = blocks(b[:, :], m), blocks(X[:, a % 2, :], m)
                mid = bb[:, :, 0, m - 1:m].to_broadcast([128, nb, m])
                V_.tensor_tensor(xx[:, :, 1, :], bb[:, :, 1, :], mid, SUB)
                V_.tensor_tensor(xx[:, :, 0, :], mid, bb[:, :, 0, :], SUB).then_inc(diff_ready, 1)

            def factors(h, a):
                m = LEVELS[a]
                xx, qq, kk = (blocks(t_, m) for t_ in (X[:, a % 2, :], qb[:, h % 2, :], fb[:, h % 2, :]))
                dve.wait_ge(exp_ready, (len(LEVELS) + 1) * h + a + 1)
                V_.tensor_tensor(xx[:, :, 1, :], xx[:, :, 1, :], qq[:, :, 1, :], MULT)
                V_.tensor_tensor(xx[:, :, 0, :], xx[:, :, 0, :], kk[:, :, 0, :], MULT).then_inc(score_in, 1)

            def take_scores(h, a):
                s = score_no(h, a)
                dve.wait_ge(score_done, s + 1)
                if s > 0:
                    dve.wait_ge(score_read, s)
                if a == 0 and h > 0:
                    dve.wait_ge(o_done, h)
                mk = masks[:, a:a + 1, :].to_broadcast([128, TT, 128])
                V_.copy_predicated(attn[:, :, :], mk, score_bank[s % 2][:, :].rearrange("p (t s) -> p t s", t=TT))\
                    .then_inc(score_read, 1)

            def piece(kind, h, a):
                if kind == "A":
                    dve.wait_ge(act_out, FN["f", h] + 1)
                    V_.tensor_scalar(fb[:, h % 2, :], fb[:, h % 2, :], lbs[:, 6, h:h + 1], lbs[:, 5, h:h + 1],
                                     MULT, ADD).then_inc(f_ready, 1)
                    dve.wait_ge(lf_ready, h + 1)
                    V_.tensor_tensor_scan(b[:, :], restart[:, :], lf, 0.0, MULT, ADD).then_inc(dve_step, 1)
                    steps[0] += 1
                    link(V_.tensor_scalar(fb[:, h % 2, :], fb[:, h % 2, :], -1.0, 1.0, MULT, ADD))
                    dve.wait_ge(act_out, FN["g", h] + 1)
                    differences(h, 0)
                if kind == "L":
                    if a + 1 < len(LEVELS):
                        differences(h, a + 1)
                    if a < len(LEVELS):
                        factors(h, a)
                    if a >= 1:
                        take_scores(h, a - 1)
                    if a == NL - 1:
                        take_scores(h, a)
                if kind == "E":
                    b3 = b[:, :].rearrange("p (c t) -> p c t", t=CHUNK)
                    last = b3[:, :, CHUNK - 1:CHUNK].to_broadcast([128, NCH, CHUNK])
                    V_.tensor_tensor(kd[:, :].rearrange("p (c t) -> p c t", t=CHUNK), last, b3, SUB)\
                        .then_inc(diff_ready, 1)
                    dve.wait_ge(exp_ready, (len(LEVELS) + 1) * (h + 1))
                    V_.tensor_tensor(kd[:, :], kd[:, :], fb[:, h % 2, :], MULT).then_inc(kd_ready, 1)
                    V_.tensor_tensor(qb[:, h % 2, :], qb[:, h % 2, :], eb[:, :], MULT).then_inc(kd_ready, 1)
                    dve.wait_ge(n_done, N["T", h] + 1)
                    V_.tensor_copy(kdT[:, :, :], n_bank[:, :].rearrange("p (t k) -> p t k", t=TT))\
                        .then_inc(kdT_ready, 1)
                if kind == "U":
                    dve.wait_ge(n_done, N["U", h] + 1)
                    for c in range(NCH - 1):
                        u = (n_bank, o_bank)[c % 2][:, 128 * (c // 2):128 * (c // 2 + 1)]
                        if c == 0:
                            ins = V_.tensor_copy(S[:, 0, :], u)
                        else:
                            ins = V_.scalar_tensor_tensor(out=S[:, c, :], in0=S[:, c - 1, :],
                                                          scalar=eb[:, CHUNK * (c + 1) - 1:CHUNK * (c + 1)],
                                                          in1=u, op0=MULT, op1=ADD)
                        ins.then_inc(S_ready, 1)
                        dve.wait_ge(S_ready, 7 * h + c + 1)
                if kind == "N":
                    inverse(("N", h), osq[:, :])
                    V_.tensor_tensor(onrm[:, :], o_bank[:, :], osq[:, :], MULT).then_inc(o_read, 1)
                    dve.wait_ge(o_read, h + 1)
                    V_.scalar_tensor_tensor(out=onrm[:, :], in0=onrm[:, :], scalar=pcol("hgn", 0),
                                            in1=gb[:, h % 2, :], op0=MULT, op1=MULT).then_inc(cat_new, 1)
                    dve.wait_ge(cat_hi, h + 1)
                    V_.tensor_tensor(cat_l[:, h, :], onrm[:, :], cat_h[:, h, :].bitcast(f32), SUB)\
                        .then_inc(cat_lo, 1)

            for at, (kind, c) in enumerate(MIX_GROUPS):
                g = G_MG + at
                src = bank[g % 4][:, :]
                dve.wait_ge(unit_used, U_MG + at + 1)
                if kind in "qfg":
                    dst = {"q": qb, "f": fb, "g": gb}[kind][:, c % 2, :]
                    if kind == "q" and c >= 2:
                        dve.wait_ge(o_done, c - 1)
                    V_.tensor_tensor(dst, src, rstd[:, :], MULT).then_inc(group_read, 1)
                elif kind in "BC":
                    dst = convB if kind == "B" else convC
                    V_.tensor_tensor(dst[:, :], src, rstd[:, :], MULT).then_inc(group_read, 1)
                else:
                    V_.tensor_tensor(convU[:, 2:], src, rstd[:, :], MULT).then_inc(group_read, 1)
                    dve.wait_ge(group_read, g + 5)
                    link(V_.tensor_tensor(convU[:, 2:], convU[:, 2:], convC[:, :], MULT))
                    w = [pcol("convw", CC * k + c) for k in range(3)]
                    link(V_.tensor_scalar(convV, convU[:, 2:], w[2], None, MULT))
                    link(V_.scalar_tensor_tensor(out=convV, in0=convU[:, 1:1 + T], scalar=w[1],
                                                 in1=convV, op0=MULT, op1=ADD))
                    link(V_.scalar_tensor_tensor(out=convV, in0=convU[:, 0:T], scalar=w[0],
                                                 in1=convV, op0=MULT, op1=ADD))
                    V_.tensor_tensor(convO[:, c, :], convV, convB[:, :], MULT).then_inc(conv_new, 1)
                    add_squares(Q_CONV + c)
                for p in PIECES.get(at, []):
                    piece(*p)
            inverse("conv", osq[:, :])
            clear()
            for c in range(CC):
                V_.scalar_tensor_tensor(out=convO[:, c, :], in0=convO[:, c, :], scalar=pcol("convn", c),
                                        in1=osq[:, :], op0=MULT, op1=MULT).then_inc(cat_new, 1)
                dve.wait_ge(cat_hi, HEADS + c + 1)
                V_.tensor_tensor(cat_l[:, HEADS + c, :], convO[:, c, :], cat_h[:, HEADS + c, :].bitcast(f32), SUB)\
                    .then_inc(cat_lo, 1)
            for k in range(KC):
                add_squares(Q_MEM + k, 0, M)
            inverse("mem", rstd[:, 0:M])
            clear()
            for k in range(KC):
                V_.scalar_tensor_tensor(out=memf[:, k, :], in0=memf[:, k, :], scalar=pcol("mem", k),
                                        in1=rstd[:, 0:M], op0=MULT, op1=MULT).then_inc(mem_norm, 1)
            for k in range(KC):
                dve.wait_ge(mem_hi, k + 1)
                V_.tensor_tensor(ml[:, k, :], memf[:, k, :], mh[:, k, :].bitcast(f32), SUB).then_inc(mem_lo, 1)
            for m in range(KC):
                update_x(m, G_WOUT, U_WOUT, 1.0)
                chunk_lo(2, m, Q_X2)
            norm_of("xa")
            for g in range(KC):
                dve.wait_ge(kv_hi, g + 1)
                V_.tensor_tensor(kTl[:, g, :], bank[(G_KT + g) % 4][:, 0:M], kTh[:, g, :].bitcast(f32), SUB)\
                    .then_inc(group_read, 1)
            for n in range(4):
                half, t = divmod(n, 2)
                cs = slice(512 * half, 512 * half + 512)
                dve.wait_ge(kv_hi, KC + n + 1)
                V_.tensor_tensor(vxl[:, t, cs], bank[(G_VX + n) % 4][:, :], vxh[:, t, cs].bitcast(f32), SUB)\
                    .then_inc(group_read, 1)
            for kind, i in XA_ORDER:
                if kind == "q":
                    g = XG["q", i]
                    dve.wait_ge(unit_used, U_WQ + i + 1)
                    V_.tensor_tensor(gbuf[:, i % 2, :], bank[g % 4][:, :], rstd[:, :], MULT).then_inc(group_read, 1)
                    dve.wait_ge(q_hi, i + 1)
                    slot = (i // 2) % 2
                    V_.tensor_tensor(ql[:, slot, i % 2, :], gbuf[:, i % 2, :], qh[:, slot, i % 2, :].bitcast(f32),
                                     SUB).then_inc(q_lo, 1)
                if kind == "S":
                    dve.wait_ge(xs_done, i + 1)
                    for n in range(2):
                        link(V_.reduce_max(smax[:, 2 * n:2 * n + 2],
                                           score_bank[n][:, :].rearrange("p (t m) -> p t m", m=M), AX.X))
                    V_.tensor_scalar(smax[:, :], smax[:, :], -1.0 / 16, None, MULT).then_inc(xmax_ready, 1)
                    dve.wait_ge(p_exp, TT * (i + 1))
                    link(V_.reciprocal(ssum[:, :], ssum[:, :]))
                    V_.tensor_tensor(P[:, :, :], P[:, :, :],
                                     ssum[:, :].rearrange("p (t a) -> p t a", a=1).to_broadcast([128, TT, M]),
                                     MULT).then_inc(p_ready, 1)
                if kind == "T":
                    for t, bk in enumerate((o_bank, n_bank)):
                        dve.wait_ge(pt_hi, 2 * i + t + 1)
                        V_.tensor_tensor(pTl[:, t, :], bk[:, :], pTh[:, t, :].bitcast(f32), SUB)\
                            .then_inc(pt_lo, 1)
                if kind == "O":
                    for d in range(2):
                        g = XG["O", i] + d
                        dve.wait_ge(cat_hi, KC + 2 * i + d + 1)
                        V_.tensor_tensor(cat_l[:, 2 * i + d, :], bank[g % 4][:, :],
                                         cat_h[:, 2 * i + d, :].bitcast(f32), SUB).then_inc(group_read, 1)
            for m in range(KC):
                update_x(m, G_WO, U_WO, 1.0)
                chunk_lo(3, m, Q_X3)
            ffn("ffn2", 1)
            inverse("final", rstd[:, :])
            for m in range(KC):
                V_.scalar_tensor_tensor(out=x[:, m, :], in0=x[:, m, :], scalar=pcol("final", m), in1=rstd[:, :],
                                        op0=MULT, op1=MULT).then_inc(cat_new, 1)

        @block.tensor
        def _(pe):
            def product(out_, a, b_, first, last, skip=False):
                nc.tensor.matmul(out_, a[0], b_[0], start=first, stop=False)
                nc.tensor.matmul(out_, a[0], b_[1], start=False, stop=False)
                return nc.tensor.matmul(out_, a[1], b_[0], start=False, stop=last)

            def wpair(slot, lo, hi_):
                return wh[:, slot, lo:hi_], wl[:, slot, lo:hi_]

            def group(u, g, off_u=None, off_g=None, x_phase=None, src=(xh, xl), cols_=T, ready=None):
                ou = 0 if off_u is None else off_u
                og = 0 if off_g is None else off_g
                slot = u % SLOTS
                pe.wait_ge(lo_ready, ou + (u + 1))
                pe.wait_ge(group_read, og + (g + 1))
                for k in range(KC):
                    if x_phase is not None:
                        pe.wait_ge(x_lo, KC * x_phase + k + 1)
                    if ready is not None:
                        if ready[1] is None:
                            pe.wait_ge(group_read, XG["O", k // 2] + k % 2 + 5)
                        else:
                            pe.wait_ge(ready[0], ready[1] + k + 1)
                    last = product(bank[g % 4][:, 0:cols_], wpair(slot, 128 * k, 128 * k + 128),
                                   (src[0][:, k, :], src[1][:, k, :]), k == 0, k == KC - 1)
                last.then_inc(unit_used, 1)

            def n_wait(name):
                if N[name] == 0:
                    return
                prev = n_uses[N[name] - 1]
                if prev[0] == "T":
                    pe.wait_ge(kdT_ready, prev[1] + 1)
                elif prev[0] == "U":
                    pe.wait_ge(S_ready, 7 * (prev[1] + 1))
                elif prev[0] == "pt":
                    pe.wait_ge(pt_lo, 2 * prev[1] + 2)
                else:
                    pe.wait_ge(rms_ready, R[prev] + 1)

            def sum_squares(name, added, width=T):
                pe.wait_ge(sq_added, added)
                n_wait(name)
                nc.tensor.matmul(n_bank[:, 0:width], ones[:, :], acc[:, 0:width], start=True, stop=True)\
                    .then_inc(n_done, 1)

            def ffn(which, norm, qn):
                u0, g0, hb = (U_FFN1, G_UP1, 0) if which == 0 else (U_FFN2, G_UP2, FC)
                ph = 0 if which == 0 else 3
                group(u0, g0, x_phase=ph)
                sum_squares(norm, qn + KC)
                for c in range(1, 4):
                    group(u0 + c, g0 + c)
                with pe.Fori(1, FC // 2) as i:
                    for c in range(4):
                        group(u0 + c, g0 + c, i * 4, i * 4)
                ud, gd, nd = u0 + N_UP, g0 + N_UP, len(DOWN_SPLIT)
                with pe.Fori(0, KC // 4) as i:
                    for m in range(4):
                        pe.wait_ge(group_read, i * 4 + (gd + m + 1))
                        j = 0
                        for c, n in enumerate(DOWN_SPLIT):
                            u = ud + m * nd + c
                            pe.wait_ge(lo_ready, i * (4 * nd) + (u + 1))
                            for k in range(n):
                                if m == 0:
                                    pe.wait_ge(hid_lo, hb + j + 1)
                                hs = slice(j * T, (j + 1) * T)
                                last = product(bank[(gd + m) % 4][:, :], wpair(u % SLOTS, 128 * k, 128 * k + 128),
                                               (hid_h[:, hs], hid_l[:, hs]), j == 0, j == FC - 1)
                                j += 1
                            last.then_inc(unit_used, 1)

            pe.wait_ge(consts_ready, 2)
            ffn(0, "ffn1", Q_X0)

            pe.wait_ge(sq_added, Q_X1 + KC)
            n_wait("mixcol")
            for t in range(TT):
                last = nc.tensor.matmul(n_bank[:, t:t + 1], acc[:, 128 * t:128 * t + 128], ones[:, 0:1],
                                        start=True, stop=True)
            last.then_inc(n_done, 1)
            for k2 in range(4):
                u = U_V + k2
                pe.wait_ge(lo_ready, u + 1)
                for t in range(TT):
                    g = G_V + t
                    if k2 == 0:
                        pe.wait_ge(group_read, g + 1)
                    for kk in range(2):
                        k = 2 * k2 + kk
                        pe.wait_ge(x_lo, KC + k + 1)
                        ts = slice(128 * t, 128 * t + 128)
                        last = product(bank[g % 4][:, :], (xh[:, k, ts], xl[:, k, ts]),
                                       wpair(u % SLOTS, 512 * kk, 512 * kk + 512), k == 0, k == KC - 1)
                last.then_inc(unit_used, 1)
                if k2 == 0:
                    sum_squares("mix", Q_X1 + KC)

            def piece(kind, h, a):
                if kind == "L":
                    s = score_no(h, a)
                    if a < len(LEVELS):
                        pe.wait_ge(score_in, len(LEVELS) * h + a + 1)
                        lhs = rhs = X[:, a % 2, :]
                    else:
                        lhs, rhs = fb[:, h % 2, :], qb[:, h % 2, :]
                    if s >= 2:
                        pe.wait_ge(score_read, s - 1)
                    for t in range(TT):
                        ts = slice(128 * t, 128 * t + 128)
                        last = nc.tensor.matmul(score_bank[s % 2][:, ts], lhs[:, ts], rhs[:, ts],
                                                start=True, stop=True)
                    last.then_inc(score_done, 1)
                if kind == "E":
                    pe.wait_ge(kd_ready, 2 * h + 1)
                    if h == 0:
                        pe.wait_ge(ident_loaded, 16)
                    n_wait(("T", h))
                    for t in range(TT):
                        ts = slice(128 * t, 128 * t + 128)
                        last = nc.tensor.transpose(n_bank[:, ts], kd[:, ts], ident[:, :])
                    last.then_inc(n_done, 1)
                if kind == "U":
                    pe.wait_ge(kdT_ready, h + 1)
                    pe.wait_ge(group_read, G_V + TT + 4)
                    n_wait(("U", h))
                    if h > 0:
                        pe.wait_ge(o_read, h)
                    for half, bk in enumerate((n_bank, o_bank)):
                        for c in range(half, NCH - 1, 2):
                            rows = slice(64 * half, 64 * half + 64)
                            last = nc.tensor.matmul(bk[:, 128 * (c // 2):128 * (c // 2 + 1)],
                                                    kdT[rows, c // 2, :], V[rows, c // 2, 128 * h:128 * h + 128],
                                                    start=True, stop=True)
                    last.then_inc(n_done, 1)
                if kind == "O":
                    pe.wait_ge(S_ready, 7 * (h + 1))
                    pe.wait_ge(score_read, NL * (h + 1))
                    for t in range(TT):
                        ts = slice(128 * t, 128 * t + 128)
                        nc.tensor.matmul(o_bank[:, ts], V[:, t, 128 * h:128 * h + 128], attn[:, t, :],
                                         start=(t == 0), stop=False, skip_group_check=True)
                    pe.wait_ge(kd_ready, 2 * (h + 1))
                    for c in range(1, NCH):
                        cs = slice(CHUNK * c, CHUNK * c + CHUNK)
                        last = nc.tensor.matmul(o_bank[:, cs], S[:, c - 1, :], qb[:, h % 2, cs],
                                                start=False, stop=(c == NCH - 1), skip_group_check=True)
                    last.then_inc(o_done, 1)
                if kind == "N":
                    pe.wait_ge(osq_ready, h + 1)
                    n_wait(("N", h))
                    nc.tensor.matmul(n_bank[:, :], ones[:, :], osq[:, :], start=True, stop=True).then_inc(n_done, 1)

            for at in range(len(MIX_GROUPS)):
                group(U_MG + at, G_MG + at)
                for p in PIECES.get(at, []):
                    piece(*p)
            sum_squares("conv", Q_CONV + CC)
            for m in range(KC):
                group(U_WOUT + m, G_WOUT + m, src=(cat_h, cat_l), ready=(cat_lo, 0) if m == 0 else None)
                if m == 1:
                    sum_squares("mem", Q_MEM + KC, M)
            for g in range(KC):
                group(U_KT + g, G_KT + g, src=(mh, ml), cols_=M, ready=(mem_lo, 0) if g == 0 else None)
                if g == 0:
                    sum_squares("xa", Q_X2 + KC)
            for half in range(2):
                for k2 in range(4):
                    u = U_VX + 4 * half + k2
                    pe.wait_ge(lo_ready, u + 1)
                    for t in range(2):
                        g = G_VX + 2 * half + t
                        if k2 == 0:
                            pe.wait_ge(group_read, g + 1)
                        for kk in range(2):
                            k = 2 * k2 + kk
                            ts = slice(128 * t, 128 * t + 128)
                            last = product(bank[g % 4][:, :], (mh[:, k, ts], ml[:, k, ts]),
                                           wpair(u % SLOTS, 512 * kk, 512 * kk + 512), k == 0, k == KC - 1)
                    last.then_inc(unit_used, 1)
            for kind, i in XA_ORDER:
                if kind == "q":
                    group(U_WQ + i, XG["q", i], x_phase=2 if i == 0 else None)
                if kind == "S":
                    pe.wait_ge(q_lo, 2 * i + 2)
                    if i == 0:
                        pe.wait_ge(group_read, G_KT + KC + 4)
                    else:
                        pe.wait_ge(p_exp, TT * i)
                    for t in range(TT):
                        ts = slice(128 * t, 128 * t + 128)
                        for d in range(2):
                            last = product(score_bank[t // 2][:, (t % 2) * M:(t % 2 + 1) * M],
                                           (qh[:, i % 2, d, ts], ql[:, i % 2, d, ts]),
                                           (kTh[:, 2 * i + d, :], kTl[:, 2 * i + d, :]), d == 0, d == 1)
                    last.then_inc(xs_done, 1)
                if kind == "T":
                    pe.wait_ge(p_ready, i + 1)
                    n_wait(("pt", i))
                    for t2, bk in enumerate((o_bank, n_bank)):
                        for t in range(TT):
                            last = nc.tensor.transpose(bk[:, 128 * t:128 * t + 128],
                                                       P[:, t, 128 * t2:128 * t2 + 128], ident[:, :])
                    last.then_inc(n_done, 1)
                if kind == "O":
                    pe.wait_ge(pt_lo, 2 * (i + 1))
                    pe.wait_ge(group_read, G_VX + 4 + 4)
                    for d in range(2):
                        g = XG["O", i] + d
                        pe.wait_ge(group_read, g + 1)
                        ds_ = slice(256 * i + 128 * d, 256 * i + 128 * d + 128)
                        for t in range(2):
                            last = product(bank[g % 4][:, :], (vxh[:, t, ds_], vxl[:, t, ds_]),
                                           (pTh[:, t, :], pTl[:, t, :]), t == 0, t == 1)
                        last.then_inc(att_done, 1)
            for m in range(KC):
                group(U_WO + m, G_WO + m, src=(cat_h, cat_l), ready=(group_read, None) if m == 0 else None)
            ffn(1, "ffn2", Q_X3)
            sum_squares("final", Q_X4 + KC)


def _pack_weights(w):
    import numpy as np

    units = np.zeros((NU, 128, UNIT), np.float32)

    def k_major(mat):
        return mat.reshape(-1, 128, mat.shape[1]).transpose(1, 0, 2).reshape(128, -1)

    def cols128(mat, c):
        return k_major(mat[:, 128 * c:128 * c + 128])

    for u0, gu, down in ((U_FFN1, w["ffn1_w_gu"][0], w["ffn1_w_down"][0]), (U_FFN2, w["ffn2_w_gu"][0], w["ffn2_w_down"][0])):
        for j in range(FC):
            units[u0 + 2 * j] = cols128(gu, j)
            units[u0 + 2 * j + 1] = cols128(gu, FC + j)
        u = u0 + N_UP
        for m in range(KC):
            whole, at = cols128(down, m), 0
            for n in DOWN_SPLIT:
                units[u, :, :128 * n] = whole[:, 128 * at:128 * (at + n)]
                at += n
                u += 1
    w_in = w["w_in"][0]
    for k2 in range(4):
        units[U_V + k2] = k_major(w_in[256 * k2:256 * k2 + 256, 1024:1536])
    first = {"q": 0, "f": 4, "g": 12, "B": 16, "C": 20, "u": 24}
    for at, (kind, c) in enumerate(MIX_GROUPS):
        units[U_MG + at] = cols128(w_in, first[kind] + c)
    for m in range(KC):
        units[U_WOUT + m] = cols128(w["w_out"][0], m)
        units[U_KT + m] = cols128(w["xa_wkv"][0], m)
        units[U_WQ + m] = cols128(w["xa_wq"][0], m)
        units[U_WO + m] = cols128(w["xa_wo"][0], m)
    for half in range(2):
        for k2 in range(4):
            units[U_VX + 4 * half + k2] = k_major(
                w["xa_wkv"][0][256 * k2:256 * k2 + 256, D + 512 * half:D + 512 * half + 512])
    return units


def _level_masks():
    import numpy as np

    s, t = np.arange(128)[:, None], np.arange(128)[None, :]
    masks = [(s // (2 * m) == t // (2 * m)) & (s % (2 * m) < m) & (t % (2 * m) >= m) for m in LEVELS]
    return np.stack(masks + [s == t], 1).reshape(128, -1).astype(np.float32)


def kernel(**inputs):
    import numpy as np
    import concourse.bacc as bacc
    from concourse.bass_utils import run_bass_kernel_spmd

    w = {n: np.asarray(a) for n, a in inputs.items()}
    x_t = np.ascontiguousarray(w["x"][0].T).reshape(KC, 128, T)
    mem_t = np.ascontiguousarray(w["mem"][0].T.reshape(KC, 128, M).transpose(1, 0, 2))

    def column(v):
        return v.reshape(-1, 128).T

    params = np.ascontiguousarray(np.concatenate([
        column(w["ffn1_norm"][0]), column(w["mix_norm"][0]), column(w["xa_norm"][0]), column(w["ffn2_norm"][0]),
        column(w["final_norm"]), column(w["mem_norm"][0]), column(w["hg_norm"][0]), column(w["conv_norm"][0]),
        column(w["conv_w"][0].reshape(-1)), column(w["lb_logits"].reshape(-1))], axis=1))
    arrays = {"w_all": _pack_weights(w), "x_t": x_t, "mem_t": mem_t, "params": params,
              "masks_d": _level_masks(), "ident_d": np.eye(128, dtype=np.float32)}
    nc = bacc.Bacc("TRN2", target_bir_lowering=False, num_devices=1)
    args = [nc.dram_tensor(n, a.shape, mybir.dt.from_np(a.dtype), kind="ExternalInput").ap() for n, a in arrays.items()]
    out = nc.dram_tensor("out_t", (KC, 128, T), mybir.dt.float32, kind="ExternalOutput").ap()
    block_kernel(nc, *args, out)
    r = run_bass_kernel_spmd(nc, [arrays], core_ids=[0])
    got = r.results[0]["out_t"]
    return np.ascontiguousarray(got.reshape(D, T).T)[None]
```

```python
import concourse.bass as bass
from concourse import mybir
from contextlib import ExitStack

D = 1024
T = 512
KC = D // 128
FF = 2816
FC = FF // 128
HEADS = 4
CC = 4
M = 256
XH = 4
CHUNK = 64
NCH = T // CHUNK
TT = T // 128
EPS = 1e-6
SLOTS = 4
UNIT = 1024
DOWN_SPLIT = [8, 8, 6]
LEVELS = [32, 16, 8, 4, 2, 1]
NL = len(LEVELS) + 1

U_FFN1 = 0
N_UP = 2 * FC
N_DOWN = KC * len(DOWN_SPLIT)
U_DOWN1 = U_FFN1 + N_UP
U_MIX = U_DOWN1 + N_DOWN
MIX_SLOTS = [("f", 0), ("q", 0), ("v", 0), ("v", 1), ("v", 2), ("v", 3),
             ("f", 1), ("q", 1), ("g", 0), ("B", 0), ("C", 0), ("u", 0),
             ("f", 2), ("q", 2), ("g", 1), ("B", 1), ("C", 1), ("u", 1),
             ("f", 3), ("q", 3), ("g", 2), ("B", 2), ("C", 2), ("u", 2), ("g", 3), ("B", 3), ("C", 3), ("u", 3)]
U_WOUT = U_MIX + len(MIX_SLOTS)
U_KT = U_WOUT + KC
XA_ORDER = [("q", 0), ("q", 1), ("vx", 0), ("S", 0), ("vx", 1), ("q", 2), ("T", 0), ("q", 3), ("O", 0),
            ("q", 4), ("S", 1), ("q", 5), ("q", 6), ("T", 1), ("S", 2), ("O", 1), ("q", 7), ("T", 2), ("S", 3), ("O", 2)]
XU = {}
_u = U_KT + KC
for _s in XA_ORDER:
    if _s[0] in ("q", "vx"):
        XU[_s] = _u
        _u += 4 if _s[0] == "vx" else 1
U_WO = _u
U_FFN2 = U_WO + KC
U_DOWN2 = U_FFN2 + N_UP
NU = U_DOWN2 + N_DOWN

PARAMS = {}
_at = 0
for _n, _w in (("ffn1", KC), ("mix", KC), ("xa", KC), ("ffn2", KC), ("final", KC), ("mem", KC),
               ("hgn", 1), ("convn", CC), ("convw", 3 * CC), ("lb", 2 * HEADS)):
    PARAMS[_n] = _at
    _at += _w
NPAR = _at

HEAD_START = [1, 7, 13, 19]
HEAD_STEPS = [("A", 0), ("L", 0), ("L", 1), ("L", 2), ("K", 0), ("Q", 0), ("S", 0), ("O", 0), ("N", 0)]
STEPS = [[(kind, h, a) for h in range(HEADS) for r, (kind, a) in enumerate(HEAD_STEPS) if HEAD_START[h] + r == at]
         for at in range(len(MIX_SLOTS))]
for _s in STEPS:
    _s.sort(key=lambda st: st[0] == "N")


def block_kernel(nc, w_all, x_t, mem_t, params, consts_mask, ident_d, out):
    f32 = mybir.dt.float32
    f32r = mybir.dt.float32r
    u8 = mybir.dt.uint8
    ALU = mybir.AluOpType
    ACT = mybir.ActivationFunctionType
    AX = mybir.AxisListType
    MULT, ADD, SUB = ALU.mult, ALU.add, ALU.subtract

    ctx = ExitStack()
    with ctx:
        def sb(name, shape, dt=f32, where=ctx):
            return where.enter_context(nc.sbuf_tensor(name, shape, dt))

        def sem(name):
            return ctx.enter_context(nc.semaphore(name))

        raw = sb("raw", [128, SLOTS, UNIT])
        wh = sb("wh", [128, SLOTS, UNIT], f32r)
        wl = sb("wl", [128, SLOTS, UNIT], f32r)
        x = sb("x", [128, KC, T])
        xh = sb("xh", [128, KC, T], f32r)
        xl = sb("xl", [128, KC, T], f32r)
        rstd = sb("rstd", [128, T])
        acc = sb("acc", [128, T])
        sq = sb("sq", [128, 2, T])
        gbuf = sb("gbuf", [128, 2, T])
        ubuf = sb("ubuf", [128, 2, T])
        convV, lf = ubuf[:, 0, :], ubuf[:, 1, :]
        half_tanh = gbuf[:, 0, :]
        ones = sb("ones", [128, 128])
        ident = sb("ident", [128, 128])
        masks = sb("masks", [128, NL, 128], u8)
        par = sb("par", [128, NPAR])
        lbs = sb("lbs", [128, 8, HEADS])
        few = sb("few", [128, 2])
        eps, one = few[:, 0:1], few[:, 1:2]
        cols = sb("cols", [128, TT])

        ffn_mem = ExitStack()
        hid_h = sb("hid_h", [128, FC * T], f32r, ffn_mem)
        hid_l = sb("hid_l", [128, FC * T], f32r, ffn_mem)
        ffn_mem.close()
        cat_h = sb("cat_h", [128, KC, T], f32r)
        cat_l = sb("cat_l", [128, KC, T], f32r)
        mix_mem = ExitStack()
        qb = sb("qb", [128, 2, T], f32, mix_mem)
        fb = sb("fb", [128, 2, T], f32, mix_mem)
        gb = sb("gb", [128, 2, T], f32, mix_mem)
        V = sb("V", [128, TT, 512], f32, mix_mem)
        b = sb("b", [128, T], f32, mix_mem)
        restart = sb("restart", [128, T], f32, mix_mem)
        X = sb("X", [128, 2, T], f32, mix_mem)
        attn = sb("attn", [128, TT, 128], f32, mix_mem)
        eb = sb("eb", [128, T], f32, mix_mem)
        kd = sb("kd", [128, T], f32, mix_mem)
        kdT = sb("kdT", [128, TT, 128], f32, mix_mem)
        S = sb("S", [128, NCH - 1, 128], f32, mix_mem)
        osq = sb("osq", [128, T], f32, mix_mem)
        onrm = sb("onrm", [128, T], f32, mix_mem)[:, :]
        convB = sb("convB", [128, T], f32, mix_mem)
        convC = sb("convC", [128, T], f32, mix_mem)
        convU = sb("convU", [128, 2 + T], f32, mix_mem)
        convO = sb("convO", [128, CC, T], f32, mix_mem)
        mix_mem.close()
        xa_mem = ExitStack()
        kTh = sb("kTh", [128, KC, M], f32r, xa_mem)
        kTl = sb("kTl", [128, KC, M], f32r, xa_mem)
        vxh = sb("vxh", [128, 2, D], f32r, xa_mem)
        vxl = sb("vxl", [128, 2, D], f32r, xa_mem)
        smax = sb("smax", [128, TT], f32, xa_mem)
        ssum = sb("ssum", [128, TT], f32, xa_mem)
        kv_mem = ExitStack()
        memf = sb("memf", [128, KC, M], f32, kv_mem)
        mh = sb("mh", [128, KC, M], f32r, kv_mem)
        ml = sb("ml", [128, KC, M], f32r, kv_mem)
        kv_mem.close()
        qhl = sb("qhl", [128, 2, 2, 2, T], f32r, xa_mem)
        pTh = sb("pTh", [128, 2, T], f32r, xa_mem)
        pTl = sb("pTl", [128, 2, T], f32r, xa_mem)
        P = ubuf[:, :, :].rearrange("p a t -> p (a t)").rearrange("p (t m) -> p t m", m=M)
        xa_mem.close()

        bank = [ctx.enter_context(nc.psum_tensor(f"bank{i}", [128, 512], f32)) for i in range(4)]
        score_bank = [ctx.enter_context(nc.psum_tensor(f"score{i}", [128, 512], f32)) for i in range(2)]
        o_bank = ctx.enter_context(nc.psum_tensor("o_bank", [128, 512], f32))
        n_bank = ctx.enter_context(nc.psum_tensor("n_bank", [128, 512], f32))

        raw_loaded = [sem(f"raw_loaded{i}") for i in range(SLOTS)]
        x_loaded = [sem(f"x_loaded{i}") for i in range(KC)]
        par_loaded = sem("par_loaded")
        mask_loaded = sem("mask_loaded")
        ident_loaded = sem("ident_loaded")
        mem_loaded = sem("mem_loaded")
        out_stored = sem("out_stored")
        hi_ready = sem("hi_ready")
        lo_ready = sem("lo_ready")
        unit_used = sem("unit_used")
        group_read = sem("group_read")
        x_hi = sem("x_hi")
        x_lo = sem("x_lo")
        sq_ready = sem("sq_ready")
        sq_added = sem("sq_added")
        acc_clear = sem("acc_clear")
        n_done = sem("n_done")
        rms_ready = sem("rms_ready")
        silu_ready = sem("silu_ready")
        hid_new = sem("hid_new")
        hid_hi = sem("hid_hi")
        hid_lo = sem("hid_lo")
        dve_step = sem("dve_step")
        consts_ready = sem("consts_ready")
        lb_diff = sem("lb_diff")
        lb_exp = sem("lb_exp")
        act_step = sem("act_step")
        lb_ready = sem("lb_ready")
        k_ready = sem("k_ready")
        act_out = sem("act_out")
        silu_done = sem("silu_done")
        lf_ready = sem("lf_ready")
        diff_ready = sem("diff_ready")
        exp_ready = sem("exp_ready")
        score_in = sem("score_in")
        score_done = sem("score_done")
        score_read = sem("score_read")
        kd_ready = sem("kd_ready")
        qd_ready = sem("qd_ready")
        kdT_ready = sem("kdT_ready")
        S_ready = sem("S_ready")
        o_done = sem("o_done")
        o_read = sem("o_read")
        osq_ready = sem("osq_ready")
        cat_new = sem("cat_new")
        cat_hi = sem("cat_hi")
        cat_lo = sem("cat_lo")
        conv_new = sem("conv_new")
        msq_ready = sem("msq_ready")
        msq_added = sem("msq_added")
        mem_norm = sem("mem_norm")
        mem_hi = sem("mem_hi")
        mem_lo = sem("mem_lo")
        kv_hi = sem("kv_hi")
        q_hi = sem("q_hi")
        q_lo = sem("q_lo")
        xs_done = sem("xs_done")
        xmax_ready = sem("xmax_ready")
        p_exp = sem("p_exp")
        p_ready = sem("p_ready")
        pt_hi = sem("pt_hi")
        pt_lo = sem("pt_lo")

        gain = {n: PARAMS[n] for n in ("ffn1", "mix", "xa", "ffn2", "final", "mem")}

        def pcol(name, i):
            return par[:, PARAMS[name] + i:PARAMS[name] + i + 1]

        DIFFS = len(LEVELS) + 1
        EXPS = DIFFS + 1
        FN = {s_: i for i, s_ in enumerate([s_ for s_ in MIX_SLOTS if s_[0] in "qfg"])}
        SN = {s_: i for i, s_ in enumerate([s_ for s_ in MIX_SLOTS if s_[0] in "qg"])}
        G_UP1 = 0
        G_DOWN1 = G_UP1 + N_UP
        G_MIX = G_DOWN1 + KC
        SLOT_GROUP, g = [], G_MIX
        for kind, i in MIX_SLOTS:
            if kind == "v":
                SLOT_GROUP.append(g - (i if i else 0))
                g += 4 if i == 0 else 0
                if i:
                    SLOT_GROUP[-1] = SLOT_GROUP[-2]
            else:
                SLOT_GROUP.append(g)
                g += 1
        G_V = SLOT_GROUP[MIX_SLOTS.index(("v", 0))]
        G_WOUT = g
        G_KT = G_WOUT + KC
        XG, g = {}, G_KT + KC
        for step in XA_ORDER:
            if step[0] in ("q", "vx"):
                XG[step] = g
                g += 2 if step[0] == "vx" else 1
        G_WO = g
        G_UP2 = G_WO + KC
        G_DOWN2 = G_UP2 + N_UP
        X_GROUP = [None, G_DOWN1, G_WOUT, G_WO, G_DOWN2]
        Q_X0, Q_X1, Q_CONV, Q_X2, Q_X3, Q_X4 = 0, 8, 16, 20, 28, 36
        n_uses = ["ffn1", "mix", "mixcol"]
        for steps_ in STEPS:
            n_uses += [(kind, h) for kind, h, _ in steps_ if kind in ("Q", "S", "N")]
        n_uses += ["conv", "mem", "xa"]
        n_uses += [(kind, i) for kind, i in XA_ORDER + [("T", 3), ("O", 3)] if kind in ("T", "O")]
        n_uses += ["ffn2", "final"]
        N = {n: i for i, n in enumerate(n_uses)}
        roots = [n for n in n_uses if isinstance(n, str) or n[0] == "N"]
        R = {n: i for i, n in enumerate(roots)}

        def score_no(h, a):
            return NL * h + a

        block = ctx.enter_context(nc.Block())

        @block.sync
        def _(sp):
            for u in range(SLOTS):
                sp.dma_start(raw[:, u, :], w_all[u, :, :]).then_inc(raw_loaded[u], 16)
                if u == 0:
                    sp.dma_start(par[:, :], params).then_inc(par_loaded, 16)
            with sp.Fori(1, NU // SLOTS) as i:
                for c in range(SLOTS):
                    sp.wait_ge(lo_ready, i * SLOTS + (c - SLOTS + 1))
                    sp.dma_start(raw[:, c, :], w_all[bass.ds(i * SLOTS + c, 1), :, :].rearrange("a p n -> p (a n)"))\
                      .then_inc(raw_loaded[c], 16)
            for m in range(KC):
                sp.wait_ge(cat_new, KC + m + 1)
                sp.dma_start(out[m, :, :], x[:, m, :]).then_inc(out_stored, 16)
            sp.wait_ge(out_stored, 16 * KC)

        @block.gpsimd
        def _(pool):
            with pool.Fori(0, NU // SLOTS) as i:
                for c in range(SLOTS):
                    pool.wait_ge(hi_ready, i * SLOTS + (c + 1))
                    nc.gpsimd.tensor_tensor(wl[:, c, :], raw[:, c, :], wh[:, c, :].bitcast(f32), SUB)\
                        .then_inc(lo_ready, 1)

        @block.scalar
        def _(act):
            def hi(u, slot=None, use=None):
                slot = u % SLOTS if slot is None else slot
                use = u // SLOTS if use is None else use
                act.wait_ge(raw_loaded[slot], (use + 1) * 16)
                if not (isinstance(u, int) and u < SLOTS):
                    act.wait_ge(unit_used, u + (1 - SLOTS))
                nc.scalar.activation(wh[:, slot, :], raw[:, slot, :], ACT.Copy).then_inc(hi_ready, 1)

            def ahead(u, i=None, base=0):
                if i is None:
                    if u + SLOTS < NU:
                        hi(u + SLOTS)
                else:
                    hi(i + (u + SLOTS), (u + SLOTS) % SLOTS, None)

            def ahead_loop(first, i4, c):
                u = first + c + SLOTS
                slot = u % SLOTS
                act.wait_ge(raw_loaded[slot], i4 * (16 // SLOTS) + 16 * (u // SLOTS + 1))
                act.wait_ge(unit_used, i4 + (u + 1 - SLOTS))
                nc.scalar.activation(wh[:, slot, :], raw[:, slot, :], ACT.Copy).then_inc(hi_ready, 1)

            def square(src, n, width=T):
                if n >= 2 if isinstance(n, int) else True:
                    act.wait_ge(sq_added, n - 1)
                slot = n % 2
                nc.scalar.activation(sq[:, slot, 0:width], src, ACT.Square).then_inc(sq_ready, 1)

            def new_x(phase, m, qn, split=True, i=None):
                off = 0 if i is None else i * 4
                chunk = m if i is None else None
                xs = x[:, m, :] if i is None else x[:, bass.ds(i * 4 + m, 1), :].rearrange("p a t -> p (a t)")
                if i is not None:
                    pass
                elif phase > 0:
                    act.wait_ge(group_read, X_GROUP[phase] + m + 5)
                else:
                    act.wait_ge(x_loaded[m], 16)
                if split:
                    name = ["ffn1", "mix", "xa", "ffn2"][phase]
                    if i is None:
                        dst, gcol = xh[:, m, :], pcol(name, m)
                    else:
                        dst = xh[:, bass.ds(i * 4 + m, 1), :].rearrange("p a t -> p (a t)")
                        gcol = par[:, bass.ds(i * 4 + (gain[name] + m), 1)]
                    nc.scalar.activation(dst, xs, ACT.Copy, scale=gcol).then_inc(x_hi, 1)
                if i is None and qn + m >= 2:
                    act.wait_ge(sq_added, qn + m - 1)
                nc.scalar.activation(sq[:, (qn + m) % 2, :], xs, ACT.Square).then_inc(sq_ready, 1)

            own = [0]

            def link(ins):
                own[0] += 1
                ins.then_inc(act_step, 1)
                act.wait_ge(act_step, own[0])

            def inverse_root(name, dst, src, width):
                act.wait_ge(n_done, N[name] + 1)
                link(nc.scalar.activation(dst, src, ACT.Ln, bias=eps, scale=1.0 / width))
                nc.scalar.activation(dst, dst, ACT.Exp, scale=-0.5).then_inc(rms_ready, 1)

            def ffn(first, last, norm, which):
                u0, g0, hb = (U_FFN1, G_UP1, 0) if which == 0 else (U_FFN2, G_UP2, FC)

                def up(i, j):
                    ahead_loop(u0, i * 4, 2 * j)
                    act.wait_ge(group_read, i * 4 + (g0 + 2 * j + 5))
                    nc.scalar.activation(gbuf[:, j, :], gbuf[:, j, :], ACT.Silu).then_inc(silu_ready, 1)
                    act.wait_ge(hid_new, i * 2 + (hb + j + 1))
                    ahead_loop(u0, i * 4, 2 * j + 1)
                    nc.scalar.activation(hid_h[:, bass.ds(i * (2 * T) + j * T, T)], ubuf[:, j, :], ACT.Copy)\
                        .then_inc(hid_hi, 1)

                act_first = True
                for j in range(2):
                    if j == 0:
                        ahead(u0)
                        inverse_root(norm, rstd[:, :], n_bank[:, :], D)
                        act.wait_ge(group_read, g0 + 2 * j + 5)
                        nc.scalar.activation(gbuf[:, j, :], gbuf[:, j, :], ACT.Silu).then_inc(silu_ready, 1)
                        ahead(u0 + 1)
                    else:
                        ahead(u0 + 2)
                        act.wait_ge(group_read, g0 + 2 * j + 5)
                        nc.scalar.activation(gbuf[:, j, :], gbuf[:, j, :], ACT.Silu).then_inc(silu_ready, 1)
                        ahead(u0 + 3)
                    act.wait_ge(hid_new, hb + j + 1)
                    nc.scalar.activation(hid_h[:, j * T:(j + 1) * T], ubuf[:, j, :], ACT.Copy).then_inc(hid_hi, 1)
                with act.Fori(1, FC // 2) as i:
                    up(i, 0)
                    up(i, 1)
                ud = u0 + N_UP
                nd = len(DOWN_SPLIT)
                phase = 1 if which == 0 else 4
                qn = Q_X1 if which == 0 else Q_X4
                if which == 0:
                    with act.Fori(0, KC // 4) as i:
                        for m in range(4):
                            for c in range(nd):
                                if c == nd - 1:
                                    act.wait_ge(group_read, i * 4 + (X_GROUP[phase] + m + 5))
                                    act.wait_ge(sq_added, i * 4 + (qn + m - 1))
                                ahead_loop(ud, i * (4 * nd), m * nd + c)
                            new_x(phase, m, qn, True, i)
                else:
                    for m in range(KC):
                        for c in range(nd):
                            ahead(ud + m * nd + c)
                        new_x(phase, m, qn, False)

            act.dma_start(x[:, 0, :], x_t[0, :, :]).then_inc(x_loaded[0], 16)
            for m in range(1, KC):
                act.dma_start(x[:, m, :], x_t[m, :, :]).then_inc(x_loaded[m], 16)
            act.dma_start(ident[:, :], ident_d).then_inc(ident_loaded, 16)
            act.dma_start(gbuf[:, :, :].rearrange("p a t -> p (a t)")[:, 0:NL * 128], consts_mask)\
               .then_inc(mask_loaded, 16)
            act.wait_ge(par_loaded, 16)
            act.wait_ge(consts_ready, 3)
            hi(0)
            for m in range(KC):
                new_x(0, m, Q_X0)
                if m < 3:
                    hi(m + 1)
            act.wait_ge(lb_diff, 1)
            nc.scalar.activation(lbs[:, 1:3, :], lbs[:, 1:3, :], ACT.Exp).then_inc(lb_exp, 1)
            ffn(0, 0, "ffn1", 0)

            def step(kind, h, a):
                f = fb[:, h % 2, :]
                if kind == "A":
                    act.wait_ge(lb_ready, 1)
                    link(nc.scalar.activation(f, f, ACT.Identity, bias=lbs[:, 5, h:h + 1], scale=lbs[:, 6, h:h + 1]))
                    nc.scalar.activation(lf, f, ACT.Ln).then_inc(lf_ready, 1)
                    nc.scalar.activation(f, f, ACT.Identity, bias=one, scale=-1.0).then_inc(k_ready, 1)
                if kind == "L":
                    for l in (2 * a, 2 * a + 1):
                        act.wait_ge(diff_ready, DIFFS * h + l + 1)
                        nc.scalar.activation(X[:, l % 2, :], X[:, l % 2, :], ACT.Exp).then_inc(exp_ready, 1)
                if kind == "K":
                    act.wait_ge(diff_ready, DIFFS * (h + 1))
                    nc.scalar.activation(kd[:, :], kd[:, :], ACT.Exp).then_inc(exp_ready, 1)
                    nc.scalar.activation(eb[:, :], b[:, :], ACT.Exp).then_inc(exp_ready, 1)
                if kind == "O":
                    act.wait_ge(o_done, h + 1)
                    nc.scalar.activation(osq[:, :], o_bank[:, :], ACT.Square).then_inc(osq_ready, 1)
                if kind == "N":
                    inverse_root(("N", h), osq[:, :], n_bank[:, :], 128)
                    act.wait_ge(cat_new, h + 1)
                    nc.scalar.activation(cat_h[:, h, :], onrm, ACT.Copy).then_inc(cat_hi, 1)

            for at, (kind, c) in enumerate(MIX_SLOTS):
                ahead(U_MIX + at)
                if at == 0:
                    inverse_root("mix", rstd[:, :], n_bank[:, :], D)
                if at == 1:
                    inverse_root("mixcol", cols[:, :], n_bank[:, 0:TT], D)
                if kind in "qfg":
                    buf = {"q": qb, "f": fb, "g": gb}[kind]
                    act.wait_ge(group_read, SLOT_GROUP[at] + 5)
                    if kind == "f":
                        nc.scalar.activation(buf[:, c % 2, :], buf[:, c % 2, :], ACT.Sigmoid).then_inc(act_out, 1)
                        act.wait_ge(act_out, FN[kind, c] + 1)
                    else:
                        nc.scalar.activation(half_tanh, buf[:, c % 2, :], ACT.Tanh).then_inc(act_out, 1)
                if kind == "u":
                    act.wait_ge(conv_new, c + 1)
                    square(convO[:, c, :], Q_CONV + c)
                for st in STEPS[at]:
                    step(*st)
            inverse_root("conv", osq[:, :], n_bank[:, :], 128 * CC)
            for c in range(CC):
                act.wait_ge(cat_new, HEADS + c + 1)
                nc.scalar.activation(cat_h[:, HEADS + c, :], convO[:, c, :], ACT.Copy).then_inc(cat_hi, 1)
            act.wait_ge(cat_lo, KC)
            act.dma_start(memf[:, :, :], mem_t).then_inc(mem_loaded, 16)
            for m in range(KC):
                ahead(U_WOUT + m)
                if m == 5:
                    inverse_root("mem", rstd[:, 0:M], n_bank[:, 0:M], D)
                    for k in range(KC):
                        act.wait_ge(mem_norm, k + 1)
                        nc.scalar.activation(mh[:, k, :], memf[:, k, :], ACT.Copy).then_inc(mem_hi, 1)
                new_x(2, m, Q_X2)
                if m == 3:
                    act.wait_ge(mem_loaded, 16)
                    for k in range(KC):
                        if k >= 2:
                            act.wait_ge(msq_added, k)
                        nc.scalar.activation(ubuf[:, k % 2, 0:M], memf[:, k, :], ACT.Square).then_inc(msq_ready, 1)
            for g in range(KC):
                ahead(U_KT + g)
                if g == 1:
                    inverse_root("xa", rstd[:, :], n_bank[:, :], D)
                act.wait_ge(unit_used, U_KT + g + 1)
                nc.scalar.activation(kTh[:, g, :], bank[(G_KT + g) % 4][:, 0:M], ACT.Copy).then_inc(kv_hi, 1)
            for kind, i in XA_ORDER + [("T", 3), ("O", 3)]:
                if kind == "q":
                    ahead(XU["q", i])
                    act.wait_ge(group_read, XG["q", i] + 5)
                    nc.scalar.activation(qhl[:, (i // 2) % 2, 0, i % 2, :], gbuf[:, i % 2, :], ACT.Copy)\
                        .then_inc(q_hi, 1)
                if kind == "vx":
                    for c in range(4):
                        ahead(XU["vx", i] + c)
                    act.wait_ge(unit_used, XU["vx", i] + 4)
                    for t in range(2):
                        nc.scalar.activation(vxh[:, t, 512 * i:512 * i + 512], bank[(XG["vx", i] + t) % 4][:, :],
                                             ACT.Copy).then_inc(kv_hi, 1)
                if kind == "S":
                    act.wait_ge(xmax_ready, i + 1)
                    if i > 0:
                        act.wait_ge(n_done, N["T", i - 1] + 1)
                    for t in range(TT):
                        nc.scalar.activation(P[:, t, :], score_bank[t // 2][:, (t % 2) * M:(t % 2 + 1) * M], ACT.Exp,
                                             bias=smax[:, t:t + 1], scale=1.0 / 16, accum_out=ssum[:, t:t + 1])\
                            .then_inc(p_exp, 1)
                if kind == "T":
                    act.wait_ge(n_done, N["T", i] + 1)
                    for t, bk in enumerate((o_bank, n_bank)):
                        nc.scalar.activation(pTh[:, t, :], bk[:, :], ACT.Copy).then_inc(pt_hi, 1)
                if kind == "O":
                    act.wait_ge(n_done, N["O", i] + 1)
                    for d, bk in enumerate((o_bank, n_bank)):
                        nc.scalar.activation(cat_h[:, 2 * i + d, :], bk[:, :], ACT.Copy).then_inc(cat_hi, 1)
            for m in range(KC):
                ahead(U_WO + m)
                new_x(3, m, Q_X3)
            ffn(0, 0, "ffn2", 1)
            inverse_root("final", rstd[:, :], n_bank[:, :], D)

        @block.vector
        def _(dve):
            steps = [0]

            def link(ins):
                steps[0] += 1
                ins.then_inc(dve_step, 1)
                dve.wait_ge(dve_step, steps[0])
                return ins

            V_ = nc.vector
            V_.memset(ones[:, :], 1.0).then_inc(consts_ready, 1)
            V_.memset(one, 1.0).then_inc(consts_ready, 1)
            V_.memset(eps, EPS).then_inc(consts_ready, 1)
            link(V_.memset(acc[:, :], 0.0))
            V_.memset(rstd[:, :], 0.0).then_inc(group_read, 4)

            dve.wait_ge(par_loaded, 16)
            l0 = par[:, PARAMS["lb"]:PARAMS["lb"] + HEADS]
            l1 = par[:, PARAMS["lb"] + HEADS:PARAMS["lb"] + 2 * HEADS]
            link(V_.tensor_tensor(lbs[:, 0, :], l0, l1, ALU.max))
            V_.tensor_tensor(lbs[:, 1, :], l0, lbs[:, 0, :], SUB)
            V_.tensor_tensor(lbs[:, 2, :], l1, lbs[:, 0, :], SUB).then_inc(lb_diff, 1)

            def chunk_lo(phase, m, qn, i=None, split=True):
                off = 0 if i is None else i * 4
                if split:
                    name = ["ffn1", "mix", "xa", "ffn2"][phase]
                    if i is None:
                        xs, dh, dl, gcol = x[:, m, :], xh[:, m, :], xl[:, m, :], pcol(name, m)
                    else:
                        xs, dh, dl = (t[:, bass.ds(i * 4 + m, 1), :].rearrange("p a t -> p (a t)") for t in (x, xh, xl))
                        gcol = par[:, bass.ds(i * 4 + (gain[name] + m), 1)]
                    dve.wait_ge(x_hi, off + (KC * phase + m + 1))
                    V_.scalar_tensor_tensor(out=dl, in0=xs, scalar=gcol, in1=dh.bitcast(f32), op0=MULT, op1=SUB)\
                        .then_inc(x_lo, 1)
                add_squares(qn + m, off)

            def add_squares(n, off=0, width=T):
                dve.wait_ge(sq_ready, off + (n + 1))
                if n > 0:
                    dve.wait_ge(sq_added, off + n)
                V_.tensor_tensor(acc[:, 0:width], acc[:, 0:width], sq[:, n % 2, 0:width], ADD).then_inc(sq_added, 1)

            def norm_of(name):
                dve.wait_ge(rms_ready, R[name] + 1)
                if name != "mix":
                    clear()

            cleared = [0]

            def clear():
                cleared[0] += 1
                V_.memset(acc[:, :], 0.0).then_inc(acc_clear, 1)
                dve.wait_ge(acc_clear, cleared[0])

            def update_x(m, g, u, scale, i=None, nd=1):
                off = 0 if i is None else i * 4
                xs = x[:, m, :] if i is None else x[:, bass.ds(i * 4 + m, 1), :].rearrange("p a t -> p (a t)")
                dve.wait_ge(unit_used, (0 if i is None else i * (4 * nd)) + (u + nd * (m + 1)))
                V_.scalar_tensor_tensor(out=xs, in0=bank[(g + m) % 4][:, :], scalar=scale, in1=xs,
                                        op0=MULT, op1=ADD).then_inc(group_read, 1)

            def ffn(norm, which):
                u0, g0, hb = (U_FFN1, G_UP1, 0) if which == 0 else (U_FFN2, G_UP2, FC)

                def up(i, j, first=False):
                    gi = 0 if first else i * 4
                    ji = 0 if first else i * 2
                    ga, gu = g0 + 2 * j, g0 + 2 * j + 1
                    dve.wait_ge(unit_used, gi + (u0 + 2 * j + 1))
                    V_.tensor_tensor(gbuf[:, j, :], bank[ga % 4][:, :], rstd[:, :], MULT).then_inc(group_read, 1)
                    dve.wait_ge(unit_used, gi + (u0 + 2 * j + 2))
                    V_.tensor_tensor(ubuf[:, j, :], bank[gu % 4][:, :], rstd[:, :], MULT).then_inc(group_read, 1)
                    dve.wait_ge(group_read, gi + (gu + 1 + 4))
                    dve.wait_ge(silu_ready, ji + (hb + j + 1))
                    V_.tensor_tensor(ubuf[:, j, :], ubuf[:, j, :], gbuf[:, j, :], MULT).then_inc(hid_new, 1)
                    dve.wait_ge(hid_hi, ji + (hb + j + 1))
                    hs = slice(j * T, (j + 1) * T) if first else bass.ds(i * (2 * T) + j * T, T)
                    V_.tensor_tensor(hid_l[:, hs], ubuf[:, j, :], hid_h[:, hs].bitcast(f32), SUB).then_inc(hid_lo, 1)

                norm_of(norm)
                up(0, 0, True)
                up(0, 1, True)
                with dve.Fori(1, FC // 2) as i:
                    up(i, 0)
                    up(i, 1)
                gd = g0 + N_UP
                if which == 0:
                    with dve.Fori(0, KC // 4) as i:
                        for m in range(4):
                            update_x(m, gd, U_DOWN1, 0.5, i, len(DOWN_SPLIT))
                            chunk_lo(1, m, Q_X1, i)
                else:
                    for m in range(KC):
                        update_x(m, gd, U_DOWN2, 0.5, None, len(DOWN_SPLIT))
                        chunk_lo(4, m, Q_X4, None, False)

            for m in range(KC):
                chunk_lo(0, m, Q_X0)
            dve.wait_ge(lb_exp, 1)
            link(V_.tensor_tensor(lbs[:, 3, :], lbs[:, 1, :], lbs[:, 2, :], ADD))
            link(V_.reciprocal(lbs[:, 4, :], lbs[:, 3, :]))
            link(V_.tensor_tensor(lbs[:, 5, :], lbs[:, 1, :], lbs[:, 4, :], MULT))
            V_.tensor_scalar(lbs[:, 6, :], lbs[:, 5, :], -1.0, 1.0, MULT, ADD).then_inc(lb_ready, 1)
            dve.wait_ge(mask_loaded, 16)
            link(V_.tensor_copy(masks[:, :, :].rearrange("p l s -> p (l s)"),
                                gbuf[:, :, :].rearrange("p a t -> p (a t)")[:, 0:NL * 128]))
            ffn("ffn1", 0)

            V_.memset(restart[:, :], 1.0).then_inc(dve_step, 1)
            steps[0] += 1
            dve.wait_ge(dve_step, steps[0])
            V_.memset(restart[:, :].rearrange("p (c t) -> p c t", t=CHUNK)[:, :, 0:1], 0.0)
            V_.memset(attn[:, :, :], 0.0)
            link(V_.memset(convU[:, 0:2], 0.0))
            norm_of("mix")

            def blocks(t_, m):
                return t_.rearrange("p (n s m) -> p n s m", s=2, m=m)

            def differences(h, a):
                m = LEVELS[a]
                nb = T // (2 * m)
                if h or a >= 2:
                    dve.wait_ge(score_done, score_no(h, a - 2) + 1 if a >= 2 else score_no(h - 1, a + 4) + 1)
                bb, xx = blocks(b[:, :], m), blocks(X[:, a % 2, :], m)
                mid = bb[:, :, 0, m - 1:m].to_broadcast([128, nb, m])
                V_.tensor_tensor(xx[:, :, 1, :], bb[:, :, 1, :], mid, SUB)
                V_.tensor_tensor(xx[:, :, 0, :], mid, bb[:, :, 0, :], SUB).then_inc(diff_ready, 1)

            def factors(h, a):
                m = LEVELS[a]
                xx, qq, kk = (blocks(t_, m) for t_ in (X[:, a % 2, :], qb[:, h % 2, :], fb[:, h % 2, :]))
                dve.wait_ge(exp_ready, EXPS * h + a + 1)
                V_.tensor_tensor(xx[:, :, 1, :], xx[:, :, 1, :], qq[:, :, 1, :], MULT)
                V_.tensor_tensor(xx[:, :, 0, :], xx[:, :, 0, :], kk[:, :, 0, :], MULT).then_inc(score_in, 1)

            def take_scores(h, a):
                s = score_no(h, a)
                dve.wait_ge(score_done, s + 1)
                if s > 0:
                    dve.wait_ge(score_read, s)
                if a == 0 and h > 0:
                    dve.wait_ge(o_done, h)
                mk = masks[:, a:a + 1, :].to_broadcast([128, TT, 128])
                V_.copy_predicated(attn[:, :, :], mk, score_bank[s % 2][:, :].rearrange("p (t s) -> p t s", t=TT))\
                    .then_inc(score_read, 1)

            def step(kind, h, a):
                if kind == "A":
                    dve.wait_ge(lf_ready, h + 1)
                    link(V_.tensor_tensor_scan(b[:, :], restart[:, :], lf, 0.0, MULT, ADD))
                if kind == "L":
                    if a == 0:
                        dve.wait_ge(k_ready, h + 1)
                        dve.wait_ge(silu_done, SN["q", h] + 1)
                    else:
                        take_scores(h, 2 * a - 2)
                        take_scores(h, 2 * a - 1)
                    differences(h, 2 * a)
                    differences(h, 2 * a + 1)
                    factors(h, 2 * a)
                    factors(h, 2 * a + 1)
                if kind == "K":
                    b3 = b[:, :].rearrange("p (c t) -> p c t", t=CHUNK)
                    last = b3[:, :, CHUNK - 1:CHUNK].to_broadcast([128, NCH, CHUNK])
                    V_.tensor_tensor(kd[:, :].rearrange("p (c t) -> p c t", t=CHUNK), last, b3, SUB)\
                        .then_inc(diff_ready, 1)
                    take_scores(h, 4)
                    take_scores(h, 5)
                    dve.wait_ge(exp_ready, EXPS * h + DIFFS)
                    V_.tensor_tensor(kd[:, :], kd[:, :], fb[:, h % 2, :], MULT).then_inc(kd_ready, 1)
                if kind == "Q":
                    take_scores(h, 6)
                    dve.wait_ge(exp_ready, EXPS * (h + 1))
                    V_.tensor_tensor(qb[:, h % 2, :], qb[:, h % 2, :], eb[:, :], MULT).then_inc(qd_ready, 1)
                    dve.wait_ge(n_done, N["Q", h] + 1)
                    V_.tensor_copy(kdT[:, :, :], n_bank[:, :].rearrange("p (t k) -> p t k", t=TT))\
                        .then_inc(kdT_ready, 1)
                if kind == "S":
                    dve.wait_ge(n_done, N["S", h] + 1)
                    for c in range(NCH - 1):
                        u = (n_bank, o_bank)[c % 2][:, 128 * (c // 2):128 * (c // 2 + 1)]
                        if c == 0:
                            ins = V_.tensor_copy(S[:, 0, :], u)
                        else:
                            ins = V_.scalar_tensor_tensor(out=S[:, c, :], in0=S[:, c - 1, :],
                                                          scalar=eb[:, CHUNK * (c + 1) - 1:CHUNK * (c + 1)],
                                                          in1=u, op0=MULT, op1=ADD)
                        ins.then_inc(S_ready, 1)
                        dve.wait_ge(S_ready, (NCH - 1) * h + c + 1)
                if kind == "N":
                    dve.wait_ge(rms_ready, R["N", h] + 1)
                    V_.tensor_tensor(onrm, o_bank[:, :], osq[:, :], MULT).then_inc(o_read, 1)
                    dve.wait_ge(o_read, h + 1)
                    dve.wait_ge(silu_done, SN["g", h] + 1)
                    V_.scalar_tensor_tensor(out=onrm, in0=onrm, scalar=pcol("hgn", 0),
                                            in1=gb[:, h % 2, :], op0=MULT, op1=MULT).then_inc(cat_new, 1)
                    dve.wait_ge(cat_hi, h + 1)
                    V_.tensor_tensor(cat_l[:, h, :], onrm, cat_h[:, h, :].bitcast(f32), SUB)\
                        .then_inc(cat_lo, 1)

            for at, (kind, c) in enumerate(MIX_SLOTS):
                g = SLOT_GROUP[at]
                src = bank[g % 4][:, :]
                if kind in "qfg":
                    dst = {"q": qb, "f": fb, "g": gb}[kind][:, c % 2, :]
                    dve.wait_ge(unit_used, U_MIX + at + 1)
                    if kind == "q" and c >= 2:
                        dve.wait_ge(o_done, c - 1)
                    if kind == "f":
                        V_.tensor_tensor(dst, src, rstd[:, :], MULT).then_inc(group_read, 1)
                    else:
                        V_.scalar_tensor_tensor(out=dst, in0=src, scalar=0.5, in1=rstd[:, :], op0=MULT, op1=MULT)\
                            .then_inc(group_read, 1)
                        dve.wait_ge(act_out, FN[kind, c] + 1)
                        V_.scalar_tensor_tensor(out=dst, in0=half_tanh, scalar=1.0, in1=dst, op0=ADD, op1=MULT)\
                            .then_inc(silu_done, 1)
                elif kind in "BC":
                    dst = convB if kind == "B" else convC
                    dve.wait_ge(unit_used, U_MIX + at + 1)
                    V_.tensor_tensor(dst[:, :], src, rstd[:, :], MULT).then_inc(group_read, 1)
                elif kind == "u":
                    dve.wait_ge(unit_used, U_MIX + at + 1)
                    V_.tensor_tensor(convU[:, 2:], src, rstd[:, :], MULT).then_inc(group_read, 1)
                    dve.wait_ge(group_read, g + 5)
                    link(V_.tensor_tensor(convU[:, 2:], convU[:, 2:], convC[:, :], MULT))
                    w = [pcol("convw", CC * k + c) for k in range(3)]
                    link(V_.tensor_scalar(convV, convU[:, 2:], w[2], None, MULT))
                    link(V_.scalar_tensor_tensor(out=convV, in0=convU[:, 1:1 + T], scalar=w[1],
                                                 in1=convV, op0=MULT, op1=ADD))
                    link(V_.scalar_tensor_tensor(out=convV, in0=convU[:, 0:T], scalar=w[0],
                                                 in1=convV, op0=MULT, op1=ADD))
                    V_.tensor_tensor(convO[:, c, :], convV, convB[:, :], MULT).then_inc(conv_new, 1)
                    add_squares(Q_CONV + c)
                elif c == 0:
                    dve.wait_ge(rms_ready, R["mixcol"] + 1)
                    clear()
                elif c == 3:
                    dve.wait_ge(unit_used, U_MIX + at + 1)
                    for t in range(TT):
                        V_.tensor_scalar(V[:, t, :], bank[(G_V + t) % 4][:, :], cols[:, t:t + 1], None, MULT)\
                            .then_inc(group_read, 1)
                for st in STEPS[at]:
                    step(*st)
            dve.wait_ge(rms_ready, R["conv"] + 1)
            clear()
            for c in range(CC):
                V_.scalar_tensor_tensor(out=convO[:, c, :], in0=convO[:, c, :], scalar=pcol("convn", c),
                                        in1=osq[:, :], op0=MULT, op1=MULT).then_inc(cat_new, 1)
                dve.wait_ge(cat_hi, HEADS + c + 1)
                V_.tensor_tensor(cat_l[:, HEADS + c, :], convO[:, c, :], cat_h[:, HEADS + c, :].bitcast(f32), SUB)\
                    .then_inc(cat_lo, 1)
            V_.memset(rstd[:, M:2 * M], 0.0).then_inc(msq_added, 1)
            for m in range(KC):
                if m == 5:
                    dve.wait_ge(rms_ready, R["mem"] + 1)
                    for k in range(KC):
                        V_.scalar_tensor_tensor(out=memf[:, k, :], in0=memf[:, k, :], scalar=pcol("mem", k),
                                                in1=rstd[:, 0:M], op0=MULT, op1=MULT).then_inc(mem_norm, 1)
                    for k in range(KC):
                        dve.wait_ge(mem_hi, k + 1)
                        V_.tensor_tensor(ml[:, k, :], memf[:, k, :], mh[:, k, :].bitcast(f32), SUB)\
                            .then_inc(mem_lo, 1)
                update_x(m, G_WOUT, U_WOUT, 1.0)
                chunk_lo(2, m, Q_X2)
                if m == 3:
                    for k in range(KC):
                        dve.wait_ge(msq_ready, k + 1)
                        dve.wait_ge(msq_added, k + 1)
                        V_.tensor_tensor(rstd[:, M:2 * M], rstd[:, M:2 * M], ubuf[:, k % 2, 0:M], ADD)\
                            .then_inc(msq_added, 1)
            norm_of("xa")
            for g in range(KC):
                dve.wait_ge(kv_hi, g + 1)
                V_.tensor_tensor(kTl[:, g, :], bank[(G_KT + g) % 4][:, 0:M], kTh[:, g, :].bitcast(f32), SUB)\
                    .then_inc(group_read, 1)
            for kind, i in XA_ORDER + [("T", 3), ("O", 3)]:
                if kind == "q":
                    g = XG["q", i]
                    dve.wait_ge(unit_used, XU["q", i] + 1)
                    V_.tensor_tensor(gbuf[:, i % 2, :], bank[g % 4][:, :], rstd[:, :], MULT).then_inc(group_read, 1)
                    dve.wait_ge(q_hi, i + 1)
                    slot = (i // 2) % 2
                    V_.tensor_tensor(qhl[:, slot, 1, i % 2, :], gbuf[:, i % 2, :], qhl[:, slot, 0, i % 2, :].bitcast(f32),
                                     SUB).then_inc(q_lo, 1)
                if kind == "vx":
                    for t in range(2):
                        cs = slice(512 * i, 512 * i + 512)
                        dve.wait_ge(kv_hi, KC + 2 * i + t + 1)
                        V_.tensor_tensor(vxl[:, t, cs], bank[(XG["vx", i] + t) % 4][:, :],
                                         vxh[:, t, cs].bitcast(f32), SUB).then_inc(group_read, 1)
                if kind == "S":
                    dve.wait_ge(xs_done, i + 1)
                    for n in range(2):
                        link(V_.reduce_max(smax[:, 2 * n:2 * n + 2],
                                           score_bank[n][:, :].rearrange("p (t m) -> p t m", m=M), AX.X))
                    V_.tensor_scalar(smax[:, :], smax[:, :], -1.0 / 16, None, MULT).then_inc(xmax_ready, 1)
                    dve.wait_ge(p_exp, TT * (i + 1))
                    link(V_.reciprocal(ssum[:, :], ssum[:, :]))
                    V_.tensor_tensor(P[:, :, :], P[:, :, :],
                                     ssum[:, :].rearrange("p (t a) -> p t a", a=1).to_broadcast([128, TT, M]),
                                     MULT).then_inc(p_ready, 1)
                if kind == "T":
                    for t, bk in enumerate((o_bank, n_bank)):
                        dve.wait_ge(pt_hi, 2 * i + t + 1)
                        V_.tensor_tensor(pTl[:, t, :], bk[:, :], pTh[:, t, :].bitcast(f32), SUB)\
                            .then_inc(pt_lo, 1)
                if kind == "O":
                    for d, bk in enumerate((o_bank, n_bank)):
                        dve.wait_ge(cat_hi, KC + 2 * i + d + 1)
                        V_.tensor_tensor(cat_l[:, 2 * i + d, :], bk[:, :], cat_h[:, 2 * i + d, :].bitcast(f32), SUB)\
                            .then_inc(cat_lo, 1)
            for m in range(KC):
                update_x(m, G_WO, U_WO, 1.0)
                chunk_lo(3, m, Q_X3)
            ffn("ffn2", 1)
            dve.wait_ge(rms_ready, R["final"] + 1)
            for m in range(KC):
                V_.scalar_tensor_tensor(out=x[:, m, :], in0=x[:, m, :], scalar=pcol("final", m), in1=rstd[:, :],
                                        op0=MULT, op1=MULT).then_inc(cat_new, 1)

        @block.tensor
        def _(pe):
            def product(out_, a, b_, first, last, skip=False):
                nc.tensor.matmul(out_, a[0], b_[0], start=first, stop=False)
                nc.tensor.matmul(out_, a[0], b_[1], start=False, stop=False)
                return nc.tensor.matmul(out_, a[1], b_[0], start=False, stop=last)

            def wpair(slot, lo, hi_):
                return wh[:, slot, lo:hi_], wl[:, slot, lo:hi_]

            def group(u, g, off_u=None, off_g=None, x_phase=None, src=(xh, xl), cols_=T, ready=None):
                ou = 0 if off_u is None else off_u
                og = 0 if off_g is None else off_g
                slot = u % SLOTS
                pe.wait_ge(lo_ready, ou + (u + 1))
                pe.wait_ge(group_read, og + (g + 1))
                for k in range(KC):
                    if x_phase is not None:
                        pe.wait_ge(x_lo, KC * x_phase + k + 1)
                    if ready is not None:
                        pe.wait_ge(ready[0], ready[1] + k + 1)
                    last = product(bank[g % 4][:, 0:cols_], wpair(slot, 128 * k, 128 * k + 128),
                                   (src[0][:, k, :], src[1][:, k, :]), k == 0, k == KC - 1)
                last.then_inc(unit_used, 1)

            def n_wait(name):
                if N[name] == 0:
                    return
                prev = n_uses[N[name] - 1]
                if prev[0] == "Q":
                    pe.wait_ge(kdT_ready, prev[1] + 1)
                elif prev[0] == "S":
                    pe.wait_ge(S_ready, (NCH - 1) * (prev[1] + 1))
                elif prev[0] == "T":
                    pe.wait_ge(pt_lo, 2 * prev[1] + 2)
                elif prev[0] == "O":
                    pe.wait_ge(cat_lo, KC + 2 * prev[1] + 2)
                else:
                    pe.wait_ge(rms_ready, R[prev] + 1)

            def sum_squares(name, added, width=T):
                pe.wait_ge(sq_added, added)
                n_wait(name)
                nc.tensor.matmul(n_bank[:, 0:width], ones[:, :], acc[:, 0:width], start=True, stop=True)\
                    .then_inc(n_done, 1)

            def ffn(which, norm, qn):
                u0, g0, hb = (U_FFN1, G_UP1, 0) if which == 0 else (U_FFN2, G_UP2, FC)
                ph = 0 if which == 0 else 3
                group(u0, g0, x_phase=ph)
                sum_squares(norm, qn + KC)
                for c in range(1, 4):
                    group(u0 + c, g0 + c)
                with pe.Fori(1, FC // 2) as i:
                    for c in range(4):
                        group(u0 + c, g0 + c, i * 4, i * 4)
                ud, gd, nd = u0 + N_UP, g0 + N_UP, len(DOWN_SPLIT)
                with pe.Fori(0, KC // 4) as i:
                    for m in range(4):
                        pe.wait_ge(group_read, i * 4 + (gd + m + 1))
                        j = 0
                        for c, n in enumerate(DOWN_SPLIT):
                            u = ud + m * nd + c
                            pe.wait_ge(lo_ready, i * (4 * nd) + (u + 1))
                            for k in range(n):
                                if m == 0:
                                    pe.wait_ge(hid_lo, hb + j + 1)
                                hs = slice(j * T, (j + 1) * T)
                                last = product(bank[(gd + m) % 4][:, :], wpair(u % SLOTS, 128 * k, 128 * k + 128),
                                               (hid_h[:, hs], hid_l[:, hs]), j == 0, j == FC - 1)
                                j += 1
                            last.then_inc(unit_used, 1)

            pe.wait_ge(consts_ready, 1)
            ffn(0, "ffn1", Q_X0)

            def step(kind, h, a):
                if kind in ("L", "K", "Q"):
                    first = {"L": 2 * a - 2, "K": 4, "Q": 6}[kind]
                    for l in range(first, min(first + 2, NL)) if first >= 0 else ():
                        s = score_no(h, l)
                        if l < len(LEVELS):
                            pe.wait_ge(score_in, len(LEVELS) * h + l + 1)
                            lhs = rhs = X[:, l % 2, :]
                        else:
                            lhs, rhs = fb[:, h % 2, :], qb[:, h % 2, :]
                        if s >= 2:
                            pe.wait_ge(score_read, s - 1)
                        for t in range(TT):
                            ts = slice(128 * t, 128 * t + 128)
                            last = nc.tensor.matmul(score_bank[s % 2][:, ts], lhs[:, ts], rhs[:, ts],
                                                    start=True, stop=True)
                        last.then_inc(score_done, 1)
                if kind == "Q":
                    pe.wait_ge(kd_ready, h + 1)
                    if h == 0:
                        pe.wait_ge(ident_loaded, 16)
                    n_wait(("Q", h))
                    for t in range(TT):
                        ts = slice(128 * t, 128 * t + 128)
                        last = nc.tensor.transpose(n_bank[:, ts], kd[:, ts], ident[:, :])
                    last.then_inc(n_done, 1)
                if kind == "S":
                    pe.wait_ge(kdT_ready, h + 1)
                    pe.wait_ge(group_read, G_V + TT + 4)
                    n_wait(("S", h))
                    if h > 0:
                        pe.wait_ge(o_read, h)
                    for half, bk in enumerate((n_bank, o_bank)):
                        for c in range(half, NCH - 1, 2):
                            rows = slice(64 * half, 64 * half + 64)
                            last = nc.tensor.matmul(bk[:, 128 * (c // 2):128 * (c // 2 + 1)],
                                                    kdT[rows, c // 2, :], V[rows, c // 2, 128 * h:128 * h + 128],
                                                    start=True, stop=True)
                    last.then_inc(n_done, 1)
                if kind == "O":
                    pe.wait_ge(S_ready, (NCH - 1) * (h + 1))
                    pe.wait_ge(score_read, NL * (h + 1))
                    for t in range(TT):
                        ts = slice(128 * t, 128 * t + 128)
                        nc.tensor.matmul(o_bank[:, ts], V[:, t, 128 * h:128 * h + 128], attn[:, t, :],
                                         start=(t == 0), stop=False, skip_group_check=True)
                    pe.wait_ge(qd_ready, h + 1)
                    for c in range(1, NCH):
                        cs = slice(CHUNK * c, CHUNK * c + CHUNK)
                        last = nc.tensor.matmul(o_bank[:, cs], S[:, c - 1, :], qb[:, h % 2, cs],
                                                start=False, stop=(c == NCH - 1), skip_group_check=True)
                    last.then_inc(o_done, 1)
                if kind == "N":
                    pe.wait_ge(osq_ready, h + 1)
                    n_wait(("N", h))
                    nc.tensor.matmul(n_bank[:, :], ones[:, :], osq[:, :], start=True, stop=True).then_inc(n_done, 1)

            for at, (kind, c) in enumerate(MIX_SLOTS):
                u = U_MIX + at
                if kind == "v":
                    pe.wait_ge(lo_ready, u + 1)
                    for t in range(TT):
                        g = G_V + t
                        if c == 0:
                            pe.wait_ge(group_read, g + 1)
                        for kk in range(2):
                            k = 2 * c + kk
                            ts = slice(128 * t, 128 * t + 128)
                            last = product(bank[g % 4][:, :], (xh[:, k, ts], xl[:, k, ts]),
                                           wpair(u % SLOTS, 512 * kk, 512 * kk + 512), k == 0, k == KC - 1)
                    last.then_inc(unit_used, 1)
                else:
                    group(u, SLOT_GROUP[at], x_phase=1 if at == 0 else None)
                if at == 0:
                    sum_squares("mix", Q_X1 + KC)
                if at == 1:
                    n_wait("mixcol")
                    for t in range(TT):
                        last = nc.tensor.matmul(n_bank[:, t:t + 1], acc[:, 128 * t:128 * t + 128], ones[:, 0:1],
                                                start=True, stop=True)
                    last.then_inc(n_done, 1)
                for st in STEPS[at]:
                    step(*st)
            def together(u0, g0, at_k, ready):
                for c in range(4):
                    pe.wait_ge(lo_ready, u0 + c + 1)
                    pe.wait_ge(group_read, g0 + c + 1)
                for k in range(KC):
                    pe.wait_ge(cat_lo, ready + k + 1)
                    for c in range(4):
                        last = product(bank[(g0 + c) % 4][:, :], wpair((u0 + c) % SLOTS, 128 * k, 128 * k + 128),
                                       (cat_h[:, k, :], cat_l[:, k, :]), k == 0, k == KC - 1)
                        if k == KC - 1:
                            last.then_inc(unit_used, 1)
                    if k in at_k:
                        at_k[k]()

            together(U_WOUT, G_WOUT, {1: lambda: sum_squares("conv", Q_CONV + CC)}, 0)
            for m in range(4, KC):
                group(U_WOUT + m, G_WOUT + m, src=(cat_h, cat_l))
                if m == 4:
                    pe.wait_ge(msq_added, KC + 1)
                    n_wait("mem")
                    nc.tensor.matmul(n_bank[:, 0:M], ones[:, :], rstd[:, M:2 * M], start=True, stop=True)\
                        .then_inc(n_done, 1)
            for g in range(KC):
                group(U_KT + g, G_KT + g, src=(mh, ml), cols_=M, ready=(mem_lo, 0) if g == 0 else None)
                if g == 1:
                    sum_squares("xa", Q_X2 + KC)
            def xa_step(kind, i):
                if kind == "q":
                    group(XU["q", i], XG["q", i], x_phase=2 if i == 0 else None)
                if kind == "vx":
                    for k2 in range(4):
                        u = XU["vx", i] + k2
                        pe.wait_ge(lo_ready, u + 1)
                        for t in range(2):
                            g = XG["vx", i] + t
                            if k2 == 0:
                                pe.wait_ge(group_read, g + 1)
                            for kk in range(2):
                                k = 2 * k2 + kk
                                ts = slice(128 * t, 128 * t + 128)
                                last = product(bank[g % 4][:, :], (mh[:, k, ts], ml[:, k, ts]),
                                               wpair(u % SLOTS, 512 * kk, 512 * kk + 512), k == 0, k == KC - 1)
                        last.then_inc(unit_used, 1)
                if kind == "S":
                    pe.wait_ge(q_lo, 2 * i + 2)
                    if i == 0:
                        pe.wait_ge(group_read, G_KT + KC + 4)
                    else:
                        pe.wait_ge(p_exp, TT * i)
                    for t in range(TT):
                        ts = slice(128 * t, 128 * t + 128)
                        for d in range(2):
                            last = product(score_bank[t // 2][:, (t % 2) * M:(t % 2 + 1) * M],
                                           (qhl[:, i % 2, 0, d, ts], qhl[:, i % 2, 1, d, ts]),
                                           (kTh[:, 2 * i + d, :], kTl[:, 2 * i + d, :]), d == 0, d == 1)
                    last.then_inc(xs_done, 1)
                if kind == "T":
                    pe.wait_ge(p_ready, i + 1)
                    n_wait(("T", i))
                    for t2, bk in enumerate((o_bank, n_bank)):
                        for t in range(TT):
                            last = nc.tensor.transpose(bk[:, 128 * t:128 * t + 128],
                                                       P[:, t, 128 * t2:128 * t2 + 128], ident[:, :])
                    last.then_inc(n_done, 1)
                if kind == "O":
                    n_wait(("O", i))
                    pe.wait_ge(group_read, XG["vx", i // 2] + 2 + 4)
                    for d, bk in enumerate((o_bank, n_bank)):
                        ds_ = slice(256 * i + 128 * d, 256 * i + 128 * d + 128)
                        for t in range(2):
                            last = product(bk[:, :], (vxh[:, t, ds_], vxl[:, t, ds_]),
                                           (pTh[:, t, :], pTl[:, t, :]), t == 0, t == 1)
                    last.then_inc(n_done, 1)

            for kind, i in XA_ORDER:
                xa_step(kind, i)
            together(U_WO, G_WO, {3: lambda: xa_step("T", 3), 5: lambda: xa_step("O", 3)}, KC)
            for m in range(4, KC):
                group(U_WO + m, G_WO + m, src=(cat_h, cat_l))
            ffn(1, "ffn2", Q_X3)
            sum_squares("final", Q_X4 + KC)


def _pack_weights(w):
    import numpy as np

    units = np.zeros((NU, 128, UNIT), np.float32)

    def k_major(mat):
        return mat.reshape(-1, 128, mat.shape[1]).transpose(1, 0, 2).reshape(128, -1)

    def cols128(mat, c):
        return k_major(mat[:, 128 * c:128 * c + 128])

    for u0, gu, down in ((U_FFN1, w["ffn1_w_gu"][0], w["ffn1_w_down"][0]), (U_FFN2, w["ffn2_w_gu"][0], w["ffn2_w_down"][0])):
        for j in range(FC):
            units[u0 + 2 * j] = cols128(gu, j)
            units[u0 + 2 * j + 1] = cols128(gu, FC + j)
        u = u0 + N_UP
        for m in range(KC):
            whole, at = cols128(down, m), 0
            for n in DOWN_SPLIT:
                units[u, :, :128 * n] = whole[:, 128 * at:128 * (at + n)]
                at += n
                u += 1
    w_in = w["w_in"][0]
    first = {"q": 0, "f": 4, "g": 12, "B": 16, "C": 20, "u": 24}
    for at, (kind, c) in enumerate(MIX_SLOTS):
        if kind == "v":
            units[U_MIX + at] = k_major(w_in[256 * c:256 * c + 256, 1024:1536])
        else:
            units[U_MIX + at] = cols128(w_in, first[kind] + c)
    for m in range(KC):
        units[U_WOUT + m] = cols128(w["w_out"][0], m)
        units[U_KT + m] = cols128(w["xa_wkv"][0], m)
        units[XU["q", m]] = cols128(w["xa_wq"][0], m)
        units[U_WO + m] = cols128(w["xa_wo"][0], m)
    for half in range(2):
        for k2 in range(4):
            units[XU["vx", half] + k2] = k_major(
                w["xa_wkv"][0][256 * k2:256 * k2 + 256, D + 512 * half:D + 512 * half + 512])
    return units


def _level_masks():
    import numpy as np

    s, t = np.arange(128)[:, None], np.arange(128)[None, :]
    masks = [(s // (2 * m) == t // (2 * m)) & (s % (2 * m) < m) & (t % (2 * m) >= m) for m in LEVELS]
    return np.stack(masks + [s == t], 1).reshape(128, -1).astype(np.float32)


def kernel(**inputs):
    import numpy as np
    import concourse.bacc as bacc
    from concourse.bass_utils import run_bass_kernel_spmd

    w = {n: np.asarray(a) for n, a in inputs.items()}
    x_t = np.ascontiguousarray(w["x"][0].T).reshape(KC, 128, T)
    mem_t = np.ascontiguousarray(w["mem"][0].T.reshape(KC, 128, M).transpose(1, 0, 2))

    def column(v):
        return v.reshape(-1, 128).T

    params = np.ascontiguousarray(np.concatenate([
        column(w["ffn1_norm"][0]), column(w["mix_norm"][0]), column(w["xa_norm"][0]), column(w["ffn2_norm"][0]),
        column(w["final_norm"]), column(w["mem_norm"][0]), column(w["hg_norm"][0]), column(w["conv_norm"][0]),
        column(w["conv_w"][0].reshape(-1)), column(w["lb_logits"].reshape(-1))], axis=1))
    arrays = {"w_all": _pack_weights(w), "x_t": x_t, "mem_t": mem_t, "params": params,
              "masks_d": _level_masks(), "ident_d": np.eye(128, dtype=np.float32)}
    nc = bacc.Bacc("TRN2", target_bir_lowering=False, num_devices=1)
    args = [nc.dram_tensor(n, a.shape, mybir.dt.from_np(a.dtype), kind="ExternalInput").ap() for n, a in arrays.items()]
    out = nc.dram_tensor("out_t", (KC, 128, T), mybir.dt.float32, kind="ExternalOutput").ap()
    block_kernel(nc, *args, out)
    r = run_bass_kernel_spmd(nc, [arrays], core_ids=[0])
    got = r.results[0]["out_t"]
    return np.ascontiguousarray(got.reshape(D, T).T)[None]
```

```python
import concourse.bass as bass
from concourse import mybir
from contextlib import ExitStack

D = 1024
T = 512
KC = D // 128
FF = 2816
FC = FF // 128
HEADS = 4
CC = 4
M = 256
XH = 4
CHUNK = 64
NCH = T // CHUNK
TT = T // 128
EPS = 1e-6
HALVES = [slice(0, T // 2), slice(T // 2, T)]
SLOTS = 4
UNIT = 1024
DOWN_SPLIT = [8, 8, 6]
LEVELS = [32, 16, 8, 4, 2, 1]
NL = len(LEVELS) + 1
MASK_COLS = 64 * len(LEVELS) + 128

U_FFN1 = 0
N_UP = 2 * FC
N_DOWN = KC * len(DOWN_SPLIT)
U_DOWN1 = U_FFN1 + N_UP
U_MIX = U_DOWN1 + N_DOWN
MIX_SLOTS = [("f", 0), ("q", 0), ("v", 0), ("v", 1), ("v", 2), ("v", 3),
             ("f", 1), ("q", 1), ("g", 0), ("B", 0), ("C", 0), ("f", 2),
             ("u", 0), ("q", 2), ("f", 3), ("g", 1), ("B", 1), ("C", 1),
             ("q", 3), ("g", 2), ("g", 3), ("u", 1), ("B", 2), ("C", 2), ("u", 2), ("B", 3), ("C", 3), ("u", 3)]
U_WOUT = U_MIX + len(MIX_SLOTS)
U_KT = U_WOUT + KC
XA_ORDER = [("q", 0), ("q", 1), ("vx", 0), ("S", 0), ("vx", 1), ("q", 2), ("T", 0), ("q", 3), ("O", 0),
            ("q", 4), ("S", 1), ("q", 5), ("q", 6), ("T", 1), ("S", 2), ("O", 1), ("q", 7), ("T", 2), ("S", 3), ("O", 2)]
XU = {}
_u = U_KT + KC
for _s in XA_ORDER:
    if _s[0] in ("q", "vx"):
        XU[_s] = _u
        _u += 4 if _s[0] == "vx" else 1
U_WO = _u
U_FFN2 = U_WO + KC
U_DOWN2 = U_FFN2 + N_UP
NU = U_DOWN2 + N_DOWN

PARAMS = {}
_at = 0
for _n, _w in (("ffn1", KC), ("mix", KC), ("xa", KC), ("ffn2", KC), ("final", KC), ("mem", KC),
               ("hgn", 1), ("convn", CC), ("convw", 3 * CC), ("lb", 2 * HEADS)):
    PARAMS[_n] = _at
    _at += _w
NPAR = _at

HEAD_START = [1, 7, 12, 17]
HEAD_STEPS = [("A", 0), ("L", 0), ("L", 1), ("L", 2), ("K", 0), ("Q", 0), ("S", 0), ("O", 0), ("N", 0)]
STEPS = [[(kind, h, a) for h in range(HEADS) for r, (kind, a) in enumerate(HEAD_STEPS) if HEAD_START[h] + r == at]
         for at in range(len(MIX_SLOTS))]
for _s in STEPS:
    _s.sort(key=lambda st: st[0] == "N")


def block_kernel(nc, w_all, x_t, mem_t, params, consts_mask, ident_d, out):
    f32 = mybir.dt.float32
    f32r = mybir.dt.float32r
    u8 = mybir.dt.uint8
    ALU = mybir.AluOpType
    ACT = mybir.ActivationFunctionType
    AX = mybir.AxisListType
    MULT, ADD, SUB = ALU.mult, ALU.add, ALU.subtract

    ctx = ExitStack()
    with ctx:
        def sb(name, shape, dt=f32, where=ctx):
            return where.enter_context(nc.sbuf_tensor(name, shape, dt))

        def sem(name):
            return ctx.enter_context(nc.semaphore(name))

        raw = sb("raw", [128, SLOTS, UNIT])
        wh = sb("wh", [128, SLOTS, UNIT], f32r)
        wl = sb("wl", [128, SLOTS, UNIT], f32r)
        x = sb("x", [128, KC, T])
        xh = sb("xh", [128, KC, T], f32r)
        xl = sb("xl", [128, KC, T], f32r)
        rstd = sb("rstd", [128, T])
        acc = sb("acc", [128, T])
        sq = sb("sq", [128, 2, T])
        gbuf = sb("gbuf", [128, 2, T])
        ubuf = sb("ubuf", [128, 2, T])
        convV, lf = ubuf[:, 0, :], ubuf[:, 1, :]
        half_tanh = gbuf[:, 0, :]
        ones = sb("ones", [128, 128])
        ident = sb("ident", [128, 128])
        masks = sb("masks", [128, MASK_COLS], u8)
        par = sb("par", [128, NPAR])
        lbs = sb("lbs", [128, 8, HEADS])
        few = sb("few", [128, 2])
        eps, one = few[:, 0:1], few[:, 1:2]
        cols = sb("cols", [128, TT])

        ffn_mem = ExitStack()
        hid_h = sb("hid_h", [128, FC * T], f32r, ffn_mem)
        hid_l = sb("hid_l", [128, FC * T], f32r, ffn_mem)
        ffn_mem.close()
        cat_h = sb("cat_h", [128, KC, T], f32r)
        cat_l = sb("cat_l", [128, KC, T], f32r)
        mix_mem = ExitStack()
        qb = sb("qb", [128, 2, T], f32, mix_mem)
        fb = sb("fb", [128, 2, T], f32, mix_mem)
        gb = sb("gb", [128, 2, T], f32, mix_mem)
        V = sb("V", [128, TT, 512], f32, mix_mem)
        b = sb("b", [128, T], f32, mix_mem)
        restart = sb("restart", [128, T], f32, mix_mem)
        X = sb("X", [128, 2, T], f32, mix_mem)
        attn = sb("attn", [128, TT, 128], f32, mix_mem)
        eb = sb("eb", [128, T], f32, mix_mem)
        kd = sb("kd", [128, T], f32, mix_mem)
        kdT = sb("kdT", [128, TT, 128], f32, mix_mem)
        S = sb("S", [128, NCH - 1, 128], f32, mix_mem)
        osq = sb("osq", [128, T], f32, mix_mem)
        onrm = sb("onrm", [128, T], f32, mix_mem)[:, :]
        convB = sb("convB", [128, T], f32, mix_mem)
        convC = sb("convC", [128, T], f32, mix_mem)
        convU = sb("convU", [128, 2 + T], f32, mix_mem)
        convO = sb("convO", [128, CC, T], f32, mix_mem)
        mix_mem.close()
        xa_mem = ExitStack()
        kTh = sb("kTh", [128, KC, M], f32r, xa_mem)
        kTl = sb("kTl", [128, KC, M], f32r, xa_mem)
        vxh = sb("vxh", [128, 2, D], f32r, xa_mem)
        vxl = sb("vxl", [128, 2, D], f32r, xa_mem)
        smax = sb("smax", [128, TT], f32, xa_mem)
        ssum = sb("ssum", [128, TT], f32, xa_mem)
        kv_mem = ExitStack()
        memf = sb("memf", [128, KC, M], f32, kv_mem)
        mh = sb("mh", [128, KC, M], f32r, kv_mem)
        ml = sb("ml", [128, KC, M], f32r, kv_mem)
        kv_mem.close()
        qhl = sb("qhl", [128, 2, 2, 2, T], f32r, xa_mem)
        pTh = sb("pTh", [128, 2, T], f32r, xa_mem)
        pTl = sb("pTl", [128, 2, T], f32r, xa_mem)
        P = ubuf[:, :, :].rearrange("p a t -> p (a t)").rearrange("p (t m) -> p t m", m=M)
        xa_mem.close()

        bank = [ctx.enter_context(nc.psum_tensor(f"bank{i}", [128, 512], f32)) for i in range(4)]
        score_bank = [ctx.enter_context(nc.psum_tensor(f"score{i}", [128, 512], f32)) for i in range(2)]
        o_bank = ctx.enter_context(nc.psum_tensor("o_bank", [128, 512], f32))
        n_bank = ctx.enter_context(nc.psum_tensor("n_bank", [128, 512], f32))

        raw_loaded = [sem(f"raw_loaded{i}") for i in range(SLOTS)]
        x_loaded = [sem(f"x_loaded{i}") for i in range(KC)]
        par_loaded = sem("par_loaded")
        mask_loaded = sem("mask_loaded")
        ident_loaded = sem("ident_loaded")
        mem_loaded = sem("mem_loaded")
        out_stored = sem("out_stored")
        half_done = sem("half_done")
        x_half = sem("x_half")
        sq_half = sem("sq_half")
        hi_ready = sem("hi_ready")
        lo_ready = sem("lo_ready")
        unit_used = sem("unit_used")
        group_read = sem("group_read")
        x_hi = sem("x_hi")
        x_lo = sem("x_lo")
        sq_ready = sem("sq_ready")
        sq_added = sem("sq_added")
        acc_clear = sem("acc_clear")
        n_done = sem("n_done")
        rms_ready = sem("rms_ready")
        silu_ready = sem("silu_ready")
        hid_new = sem("hid_new")
        hid_hi = sem("hid_hi")
        hid_lo = sem("hid_lo")
        dve_step = sem("dve_step")
        consts_ready = sem("consts_ready")
        lb_diff = sem("lb_diff")
        lb_exp = sem("lb_exp")
        act_step = sem("act_step")
        lb_ready = sem("lb_ready")
        k_ready = sem("k_ready")
        act_out = sem("act_out")
        silu_done = sem("silu_done")
        lf_ready = sem("lf_ready")
        diff_ready = sem("diff_ready")
        exp_ready = sem("exp_ready")
        score_in = sem("score_in")
        score_done = sem("score_done")
        score_read = sem("score_read")
        kd_ready = sem("kd_ready")
        qd_ready = sem("qd_ready")
        kdT_ready = sem("kdT_ready")
        S_ready = sem("S_ready")
        o_done = sem("o_done")
        o_read = sem("o_read")
        osq_ready = sem("osq_ready")
        cat_new = sem("cat_new")
        cat_hi = sem("cat_hi")
        cat_lo = sem("cat_lo")
        conv_new = sem("conv_new")
        msq_ready = sem("msq_ready")
        msq_added = sem("msq_added")
        mem_norm = sem("mem_norm")
        mem_hi = sem("mem_hi")
        mem_lo = sem("mem_lo")
        kv_hi = sem("kv_hi")
        q_hi = sem("q_hi")
        q_lo = sem("q_lo")
        xs_done = sem("xs_done")
        xmax_ready = sem("xmax_ready")
        p_exp = sem("p_exp")
        p_ready = sem("p_ready")
        pt_hi = sem("pt_hi")
        pt_lo = sem("pt_lo")

        gain = {n: PARAMS[n] for n in ("ffn1", "mix", "xa", "ffn2", "final", "mem")}

        def pcol(name, i):
            return par[:, PARAMS[name] + i:PARAMS[name] + i + 1]

        DIFFS = len(LEVELS) + 1
        EXPS = DIFFS + 1
        FN = {s_: i for i, s_ in enumerate([s_ for s_ in MIX_SLOTS if s_[0] in "qfg"])}
        SN = {s_: i for i, s_ in enumerate([s_ for s_ in MIX_SLOTS if s_[0] in "qg"])}
        G_UP1 = 0
        G_DOWN1 = G_UP1 + N_UP
        G_MIX = G_DOWN1 + KC
        SLOT_GROUP, g = [], G_MIX
        for kind, i in MIX_SLOTS:
            if kind == "v":
                SLOT_GROUP.append(g - (i if i else 0))
                g += 4 if i == 0 else 0
                if i:
                    SLOT_GROUP[-1] = SLOT_GROUP[-2]
            else:
                SLOT_GROUP.append(g)
                g += 1
        G_V = SLOT_GROUP[MIX_SLOTS.index(("v", 0))]
        G_WOUT = g
        G_KT = G_WOUT + KC
        XG, g = {}, G_KT + KC
        for step in XA_ORDER:
            if step[0] in ("q", "vx"):
                XG[step] = g
                g += 2 if step[0] == "vx" else 1
        G_WO = g
        G_UP2 = G_WO + KC
        G_DOWN2 = G_UP2 + N_UP
        X_GROUP = [None, G_DOWN1, G_WOUT, G_WO, G_DOWN2]
        Q_X0, Q_X1, Q_CONV, Q_X2, Q_X3, Q_X4 = 0, 8, 16, 20, 28, 36
        n_uses = ["ffn1", "mix", "mixcol"]
        for steps_ in STEPS:
            n_uses += [(kind, h) for kind, h, _ in steps_ if kind in ("Q", "S", "N")]
        n_uses += ["conv", "mem", "xa"]
        n_uses += [(kind, i) for kind, i in XA_ORDER + [("T", 3), ("O", 3)] if kind in ("T", "O")]
        n_uses += ["ffn2", "final"]
        N = {n: i for i, n in enumerate(n_uses)}
        roots = [n for n in n_uses if isinstance(n, str) or n[0] == "N"]
        R = {n: i for i, n in enumerate(roots)}

        def score_no(h, a):
            return NL * h + a

        block = ctx.enter_context(nc.Block())

        @block.sync
        def _(sp):
            sp.dma_start(raw[:, 0, :], w_all[0, :, :]).then_inc(raw_loaded[0], 16)
            sp.dma_start(par[:, :], params).then_inc(par_loaded, 16)
            for m in range(KC):
                sp.dma_start(x[:, m, :], x_t[m, :, :]).then_inc(x_loaded[m], 16)
            for u in range(1, SLOTS):
                sp.dma_start(raw[:, u, :], w_all[u, :, :]).then_inc(raw_loaded[u], 16)
            sp.dma_start(gbuf[:, :, :].rearrange("p a t -> p (a t)")[:, 0:MASK_COLS], consts_mask)\
              .then_inc(mask_loaded, 16)
            sp.dma_start(ident[:, :], ident_d).then_inc(ident_loaded, 16)
            with sp.Fori(1, NU // SLOTS) as i:
                for c in range(SLOTS):
                    sp.wait_ge(lo_ready, i * SLOTS + (c - SLOTS + 1))
                    sp.dma_start(raw[:, c, :], w_all[bass.ds(i * SLOTS + c, 1), :, :].rearrange("a p n -> p (a n)"))\
                      .then_inc(raw_loaded[c], 16)
            for h in range(2):
                for m in range(0, KC, 2):
                    sp.wait_ge(cat_new, KC + KC * h + m + 2)
                    sp.dma_start(out[m:m + 2, :, HALVES[h]].rearrange("a p t -> p a t"), x[:, m:m + 2, HALVES[h]])\
                      .then_inc(out_stored, 16)
            sp.wait_ge(out_stored, 16 * KC)

        @block.gpsimd
        def _(pool):
            with pool.Fori(0, NU // SLOTS) as i:
                for c in range(SLOTS):
                    pool.wait_ge(hi_ready, i * SLOTS + (c + 1))
                    nc.gpsimd.tensor_tensor(wl[:, c, :], raw[:, c, :], wh[:, c, :].bitcast(f32), SUB)\
                        .then_inc(lo_ready, 1)

        @block.scalar
        def _(act):
            def hi(u):
                slot = u % SLOTS
                act.wait_ge(raw_loaded[slot], (u // SLOTS + 1) * 16)
                if u >= SLOTS:
                    act.wait_ge(unit_used, u + 1 - SLOTS)
                nc.scalar.activation(wh[:, slot, :], raw[:, slot, :], ACT.Copy).then_inc(hi_ready, 1)

            def ahead(u):
                if u + SLOTS < NU:
                    hi(u + SLOTS)

            def ahead_loop(first, i4, c):
                u = first + c + SLOTS
                slot = u % SLOTS
                act.wait_ge(raw_loaded[slot], i4 * (16 // SLOTS) + 16 * (u // SLOTS + 1))
                act.wait_ge(unit_used, i4 + (u + 1 - SLOTS))
                nc.scalar.activation(wh[:, slot, :], raw[:, slot, :], ACT.Copy).then_inc(hi_ready, 1)

            def square(src, n):
                if n >= 2:
                    act.wait_ge(sq_added, n - 1)
                nc.scalar.activation(sq[:, n % 2, :], src, ACT.Square).then_inc(sq_ready, 1)

            def new_x(phase, m, qn, split=True, i=None):
                xs = x[:, m, :] if i is None else x[:, bass.ds(i * 4 + m, 1), :].rearrange("p a t -> p (a t)")
                if i is None:
                    act.wait_ge(group_read, X_GROUP[phase] + m + 5)
                if split:
                    name = ["ffn1", "mix", "xa", "ffn2"][phase]
                    if i is None:
                        dst, gcol = xh[:, m, :], pcol(name, m)
                    else:
                        dst = xh[:, bass.ds(i * 4 + m, 1), :].rearrange("p a t -> p (a t)")
                        gcol = par[:, bass.ds(i * 4 + (gain[name] + m), 1)]
                    nc.scalar.activation(dst, xs, ACT.Copy, scale=gcol).then_inc(x_hi, 1)
                if i is None and qn + m >= 2:
                    act.wait_ge(sq_added, qn + m - 1)
                nc.scalar.activation(sq[:, (qn + m) % 2, :], xs, ACT.Square).then_inc(sq_ready, 1)

            own = [0]

            def link(ins):
                own[0] += 1
                ins.then_inc(act_step, 1)
                act.wait_ge(act_step, own[0])

            def inverse_root(name, dst, src, width):
                act.preload_act_table_set("natural_log_exp_and_others")
                act.wait_ge(n_done, N[name] + 1)
                link(nc.scalar.activation(dst, src, ACT.Ln, bias=eps, scale=1.0 / width))
                nc.scalar.activation(dst, dst, ACT.Exp, scale=-0.5).then_inc(rms_ready, 1)

            def ffn(norm, which):
                u0, g0, hb = (U_FFN1, G_UP1, 0) if which == 0 else (U_FFN2, G_UP2, FC)

                def up(i, j):
                    ahead_loop(u0, i * 4, 2 * j)
                    act.wait_ge(group_read, i * 4 + (g0 + 2 * j + 5))
                    nc.scalar.activation(gbuf[:, j, :], gbuf[:, j, :], ACT.Silu).then_inc(silu_ready, 1)
                    act.wait_ge(hid_new, i * 2 + (hb + j + 1))
                    ahead_loop(u0, i * 4, 2 * j + 1)
                    nc.scalar.activation(hid_h[:, bass.ds(i * (2 * T) + j * T, T)], ubuf[:, j, :], ACT.Copy)\
                        .then_inc(hid_hi, 1)

                for j in range(2):
                    if j == 0:
                        ahead(u0)
                        inverse_root(norm, rstd[:, :], n_bank[:, :], D)
                        act.wait_ge(group_read, g0 + 2 * j + 5)
                        nc.scalar.activation(gbuf[:, j, :], gbuf[:, j, :], ACT.Silu).then_inc(silu_ready, 1)
                        ahead(u0 + 1)
                    else:
                        ahead(u0 + 2)
                        act.wait_ge(group_read, g0 + 2 * j + 5)
                        nc.scalar.activation(gbuf[:, j, :], gbuf[:, j, :], ACT.Silu).then_inc(silu_ready, 1)
                        ahead(u0 + 3)
                    act.wait_ge(hid_new, hb + j + 1)
                    nc.scalar.activation(hid_h[:, j * T:(j + 1) * T], ubuf[:, j, :], ACT.Copy).then_inc(hid_hi, 1)
                with act.Fori(1, FC // 2) as i:
                    up(i, 0)
                    up(i, 1)
                ud = u0 + N_UP
                nd = len(DOWN_SPLIT)
                phase = 1 if which == 0 else 4
                qn = Q_X1 if which == 0 else Q_X4
                if which == 0:
                    with act.Fori(0, KC // 4) as i:
                        for m in range(4):
                            for c in range(nd):
                                if c == nd - 1:
                                    act.wait_ge(group_read, i * 4 + (X_GROUP[phase] + m + 5))
                                    act.wait_ge(sq_added, i * 4 + (qn + m - 1))
                                ahead_loop(ud, i * (4 * nd), m * nd + c)
                            new_x(phase, m, qn, True, i)
                else:
                    for m in range(KC):
                        for c in range(nd):
                            ahead(ud + m * nd + c)
                        if m < KC - 1:
                            new_x(phase, m, qn, False)

            act.preload_act_table_set("natural_log_exp_and_others")
            act.wait_ge(par_loaded, 16)
            for m in range(KC):
                act.wait_ge(x_loaded[m], 16)
                nc.scalar.activation(xh[:, m, :], x[:, m, :], ACT.Copy, scale=pcol("ffn1", m)).then_inc(x_hi, 1)
            act.wait_ge(hi_ready, 1)
            hi(1)
            for m in range(KC):
                if m in (2, 5):
                    hi(2 + m // 4)
                square(x[:, m, :], Q_X0 + m)
            act.wait_ge(consts_ready, 3)
            act.wait_ge(lb_diff, 1)
            nc.scalar.activation(lbs[:, 1:3, :], lbs[:, 1:3, :], ACT.Exp).then_inc(lb_exp, 1)
            ffn("ffn1", 0)

            def step(kind, h, a):
                f = fb[:, h % 2, :]
                if kind == "A":
                    act.preload_act_table_set("natural_log_exp_and_others")
                    act.wait_ge(lb_ready, 1)
                    link(nc.scalar.activation(f, f, ACT.Identity, bias=lbs[:, 5, h:h + 1], scale=lbs[:, 6, h:h + 1]))
                    nc.scalar.activation(lf, f, ACT.Ln).then_inc(lf_ready, 1)
                    nc.scalar.activation(f, f, ACT.Identity, bias=one, scale=-1.0).then_inc(k_ready, 1)
                if kind == "L":
                    for l in (2 * a, 2 * a + 1):
                        act.wait_ge(diff_ready, DIFFS * h + l + 1)
                        nc.scalar.activation(X[:, l % 2, :], X[:, l % 2, :], ACT.Exp).then_inc(exp_ready, 1)
                if kind == "K":
                    act.wait_ge(diff_ready, DIFFS * (h + 1))
                    nc.scalar.activation(kd[:, :], kd[:, :], ACT.Exp).then_inc(exp_ready, 1)
                    nc.scalar.activation(eb[:, :], b[:, :], ACT.Exp).then_inc(exp_ready, 1)
                if kind == "O":
                    act.wait_ge(o_done, h + 1)
                    nc.scalar.activation(osq[:, :], o_bank[:, :], ACT.Square).then_inc(osq_ready, 1)
                if kind == "N":
                    inverse_root(("N", h), osq[:, :], n_bank[:, :], 128)
                    act.wait_ge(cat_new, h + 1)
                    nc.scalar.activation(cat_h[:, h, :], onrm, ACT.Copy).then_inc(cat_hi, 1)

            for at, (kind, c) in enumerate(MIX_SLOTS):
                if at == 0:
                    inverse_root("mix", rstd[:, :], n_bank[:, :], D)
                if at == 1:
                    inverse_root("mixcol", cols[:, :], n_bank[:, 0:TT], D)
                if kind in "qfg":
                    buf = {"q": qb, "f": fb, "g": gb}[kind]
                    act.wait_ge(group_read, SLOT_GROUP[at] + 5)
                    if kind == "f":
                        nc.scalar.activation(buf[:, c % 2, :], buf[:, c % 2, :], ACT.Sigmoid).then_inc(act_out, 1)
                        act.wait_ge(act_out, FN[kind, c] + 1)
                    else:
                        nc.scalar.activation(half_tanh, buf[:, c % 2, :], ACT.Tanh).then_inc(act_out, 1)
                ahead(U_MIX + at)
                for st in STEPS[at]:
                    step(*st)
                if kind == "u":
                    act.wait_ge(conv_new, c + 1)
                    square(convO[:, c, :], Q_CONV + c)
            inverse_root("conv", osq[:, :], n_bank[:, :], 128 * CC)
            for c in range(CC):
                act.wait_ge(cat_new, HEADS + c + 1)
                nc.scalar.activation(cat_h[:, HEADS + c, :], convO[:, c, :], ACT.Copy).then_inc(cat_hi, 1)
            act.wait_ge(cat_lo, KC)
            act.dma_start(memf[:, :, :], mem_t).then_inc(mem_loaded, 16)
            for m in range(KC):
                if m == 4:
                    inverse_root("mem", rstd[:, 0:M], n_bank[:, 0:M], D)
                    for k in range(KC):
                        act.wait_ge(mem_norm, k + 1)
                        nc.scalar.activation(mh[:, k, :], memf[:, k, :], ACT.Copy).then_inc(mem_hi, 1)
                ahead(U_WOUT + m)
                if m == 1:
                    act.wait_ge(mem_loaded, 16)
                    for k in range(KC):
                        if k >= 2:
                            act.wait_ge(msq_added, k)
                        nc.scalar.activation(ubuf[:, k % 2, 0:M], memf[:, k, :], ACT.Square).then_inc(msq_ready, 1)
                new_x(2, m, Q_X2)
            for g in range(KC):
                ahead(U_KT + g)
                if g == 3:
                    inverse_root("xa", rstd[:, :], n_bank[:, :], D)
                act.wait_ge(unit_used, U_KT + g + 1)
                nc.scalar.activation(kTh[:, g, :], bank[(G_KT + g) % 4][:, 0:M], ACT.Copy).then_inc(kv_hi, 1)
            for kind, i in XA_ORDER + [("T", 3), ("O", 3)]:
                if kind == "q":
                    act.wait_ge(group_read, XG["q", i] + 5)
                    nc.scalar.activation(qhl[:, (i // 2) % 2, 0, i % 2, :], gbuf[:, i % 2, :], ACT.Copy)\
                        .then_inc(q_hi, 1)
                    ahead(XU["q", i])
                if kind == "vx":
                    for c in range(4):
                        ahead(XU["vx", i] + c)
                    act.wait_ge(unit_used, XU["vx", i] + 4)
                    for t in range(2):
                        nc.scalar.activation(vxh[:, t, 512 * i:512 * i + 512], bank[(XG["vx", i] + t) % 4][:, :],
                                             ACT.Copy).then_inc(kv_hi, 1)
                if kind == "S":
                    act.wait_ge(xmax_ready, i + 1)
                    if i > 0:
                        act.wait_ge(n_done, N["T", i - 1] + 1)
                    for t in range(TT):
                        nc.scalar.activation(P[:, t, :], score_bank[t // 2][:, (t % 2) * M:(t % 2 + 1) * M], ACT.Exp,
                                             bias=smax[:, t:t + 1], scale=1.0 / 16, accum_out=ssum[:, t:t + 1])\
                            .then_inc(p_exp, 1)
                if kind == "T":
                    act.wait_ge(n_done, N["T", i] + 1)
                    for t, bk in enumerate((o_bank, n_bank)):
                        nc.scalar.activation(pTh[:, t, :], bk[:, :], ACT.Copy).then_inc(pt_hi, 1)
                if kind == "O":
                    act.wait_ge(n_done, N["O", i] + 1)
                    for d, bk in enumerate((o_bank, n_bank)):
                        nc.scalar.activation(cat_h[:, 2 * i + d, :], bk[:, :], ACT.Copy).then_inc(cat_hi, 1)
            for m in range(KC):
                ahead(U_WO + m)
                new_x(3, m, Q_X3)
            ffn("ffn2", 1)
            act.preload_act_table_set("natural_log_exp_and_others")
            act.wait_ge(sq_added, Q_X4 + KC - 2)
            for h, bk in enumerate((n_bank, o_bank)):
                act.wait_ge(x_half, h + 1)
                nc.scalar.activation(sq[:, 1, HALVES[h]], x[:, KC - 1, HALVES[h]], ACT.Square).then_inc(sq_half, 1)
                act.wait_ge(n_done, N["final"] + h + 1)
                link(nc.scalar.activation(rstd[:, HALVES[h]], bk[:, HALVES[h]], ACT.Ln, bias=eps, scale=1.0 / D))
                nc.scalar.activation(rstd[:, HALVES[h]], rstd[:, HALVES[h]], ACT.Exp, scale=-0.5).then_inc(rms_ready, 1)

        @block.vector
        def _(dve):
            steps = [0]

            def link(ins):
                steps[0] += 1
                ins.then_inc(dve_step, 1)
                dve.wait_ge(dve_step, steps[0])
                return ins

            V_ = nc.vector
            V_.memset(ones[:, :], 1.0).then_inc(consts_ready, 1)
            V_.memset(one, 1.0).then_inc(consts_ready, 1)
            V_.memset(eps, EPS).then_inc(consts_ready, 1)
            link(V_.memset(acc[:, :], 0.0))
            V_.memset(rstd[:, :], 0.0).then_inc(group_read, 4)

            dve.wait_ge(raw_loaded[0], 16)
            V_.tensor_copy(wh[:, 0, :], raw[:, 0, :]).then_inc(hi_ready, 1)
            dve.wait_ge(par_loaded, 16)
            l0 = par[:, PARAMS["lb"]:PARAMS["lb"] + HEADS]
            l1 = par[:, PARAMS["lb"] + HEADS:PARAMS["lb"] + 2 * HEADS]
            link(V_.tensor_tensor(lbs[:, 0, :], l0, l1, ALU.max))
            V_.tensor_tensor(lbs[:, 1, :], l0, lbs[:, 0, :], SUB)
            V_.tensor_tensor(lbs[:, 2, :], l1, lbs[:, 0, :], SUB).then_inc(lb_diff, 1)

            def chunk_lo(phase, m, qn, i=None, split=True):
                off = 0 if i is None else i * 4
                if split:
                    name = ["ffn1", "mix", "xa", "ffn2"][phase]
                    if i is None:
                        xs, dh, dl, gcol = x[:, m, :], xh[:, m, :], xl[:, m, :], pcol(name, m)
                    else:
                        xs, dh, dl = (t[:, bass.ds(i * 4 + m, 1), :].rearrange("p a t -> p (a t)") for t in (x, xh, xl))
                        gcol = par[:, bass.ds(i * 4 + (gain[name] + m), 1)]
                    dve.wait_ge(x_hi, off + (KC * phase + m + 1))
                    V_.scalar_tensor_tensor(out=dl, in0=xs, scalar=gcol, in1=dh.bitcast(f32), op0=MULT, op1=SUB)\
                        .then_inc(x_lo, 1)
                add_squares(qn + m, off)

            def add_squares(n, off=0):
                dve.wait_ge(sq_ready, off + (n + 1))
                if n > 0:
                    dve.wait_ge(sq_added, off + n)
                V_.tensor_tensor(acc[:, :], acc[:, :], sq[:, n % 2, :], ADD).then_inc(sq_added, 1)

            def norm_of(name):
                dve.wait_ge(rms_ready, R[name] + 1)
                if name != "mix":
                    clear()

            cleared = [0]

            def clear():
                cleared[0] += 1
                V_.memset(acc[:, :], 0.0).then_inc(acc_clear, 1)
                dve.wait_ge(acc_clear, cleared[0])

            def update_x(m, g, u, scale, i=None, nd=1):
                off = 0 if i is None else i * 4
                xs = x[:, m, :] if i is None else x[:, bass.ds(i * 4 + m, 1), :].rearrange("p a t -> p (a t)")
                dve.wait_ge(unit_used, (0 if i is None else i * (4 * nd)) + (u + nd * (m + 1)))
                V_.scalar_tensor_tensor(out=xs, in0=bank[(g + m) % 4][:, :], scalar=scale, in1=xs,
                                        op0=MULT, op1=ADD).then_inc(group_read, 1)

            def ffn(norm, which):
                u0, g0, hb = (U_FFN1, G_UP1, 0) if which == 0 else (U_FFN2, G_UP2, FC)

                def up(i, j, first=False):
                    gi = 0 if first else i * 4
                    ji = 0 if first else i * 2
                    ga, gu = g0 + 2 * j, g0 + 2 * j + 1
                    dve.wait_ge(unit_used, gi + (u0 + 2 * j + 1))
                    V_.tensor_tensor(gbuf[:, j, :], bank[ga % 4][:, :], rstd[:, :], MULT).then_inc(group_read, 1)
                    dve.wait_ge(unit_used, gi + (u0 + 2 * j + 2))
                    V_.tensor_tensor(ubuf[:, j, :], bank[gu % 4][:, :], rstd[:, :], MULT).then_inc(group_read, 1)
                    dve.wait_ge(group_read, gi + (gu + 1 + 4))
                    dve.wait_ge(silu_ready, ji + (hb + j + 1))
                    V_.tensor_tensor(ubuf[:, j, :], ubuf[:, j, :], gbuf[:, j, :], MULT).then_inc(hid_new, 1)
                    dve.wait_ge(hid_hi, ji + (hb + j + 1))
                    hs = slice(j * T, (j + 1) * T) if first else bass.ds(i * (2 * T) + j * T, T)
                    V_.tensor_tensor(hid_l[:, hs], ubuf[:, j, :], hid_h[:, hs].bitcast(f32), SUB).then_inc(hid_lo, 1)

                norm_of(norm)
                up(0, 0, True)
                up(0, 1, True)
                with dve.Fori(1, FC // 2) as i:
                    up(i, 0)
                    up(i, 1)
                gd = g0 + N_UP
                if which == 0:
                    with dve.Fori(0, KC // 4) as i:
                        for m in range(4):
                            update_x(m, gd, U_DOWN1, 0.5, i, len(DOWN_SPLIT))
                            chunk_lo(1, m, Q_X1, i)
                else:
                    for m in range(KC - 1):
                        update_x(m, gd, U_DOWN2, 0.5, None, len(DOWN_SPLIT))
                        chunk_lo(4, m, Q_X4, None, False)

            for m in range(KC):
                dve.wait_ge(x_hi, m + 1)
                V_.scalar_tensor_tensor(out=xl[:, m, :], in0=x[:, m, :], scalar=pcol("ffn1", m),
                                        in1=xh[:, m, :].bitcast(f32), op0=MULT, op1=SUB).then_inc(x_lo, 1)
            for m in range(KC):
                add_squares(Q_X0 + m)
            dve.wait_ge(lb_exp, 1)
            link(V_.tensor_tensor(lbs[:, 3, :], lbs[:, 1, :], lbs[:, 2, :], ADD))
            link(V_.reciprocal(lbs[:, 4, :], lbs[:, 3, :]))
            link(V_.tensor_tensor(lbs[:, 5, :], lbs[:, 1, :], lbs[:, 4, :], MULT))
            V_.tensor_scalar(lbs[:, 6, :], lbs[:, 5, :], -1.0, 1.0, MULT, ADD).then_inc(lb_ready, 1)
            dve.wait_ge(mask_loaded, 16)
            link(V_.tensor_copy(masks[:, :], gbuf[:, :, :].rearrange("p a t -> p (a t)")[:, 0:MASK_COLS]))
            ffn("ffn1", 0)

            link(V_.memset(restart[:, :], 1.0))
            V_.memset(restart[:, :].rearrange("p (c t) -> p c t", t=CHUNK)[:, :, 0:1], 0.0)
            V_.memset(attn[:, :, :], 0.0)
            link(V_.memset(convU[:, 0:2], 0.0))
            norm_of("mix")

            def blocks(t_, m):
                return t_.rearrange("p (n s m) -> p n s m", s=2, m=m)

            def differences(h, a):
                m = LEVELS[a]
                nb = T // (2 * m)
                if h or a >= 2:
                    dve.wait_ge(score_done, score_no(h, a - 2) + 1 if a >= 2 else score_no(h - 1, a + 4) + 1)
                bb, xx = blocks(b[:, :], m), blocks(X[:, a % 2, :], m)
                mid = bb[:, :, 0, m - 1:m].to_broadcast([128, nb, m])
                V_.tensor_tensor(xx[:, :, 1, :], bb[:, :, 1, :], mid, SUB)
                V_.tensor_tensor(xx[:, :, 0, :], mid, bb[:, :, 0, :], SUB).then_inc(diff_ready, 1)

            def factors(h, a):
                m = LEVELS[a]
                xx, qq, kk = (blocks(t_, m) for t_ in (X[:, a % 2, :], qb[:, h % 2, :], fb[:, h % 2, :]))
                dve.wait_ge(exp_ready, EXPS * h + a + 1)
                V_.tensor_tensor(xx[:, :, 1, :], xx[:, :, 1, :], qq[:, :, 1, :], MULT)
                V_.tensor_tensor(xx[:, :, 0, :], xx[:, :, 0, :], kk[:, :, 0, :], MULT).then_inc(score_in, 1)

            def take_scores(h, a):
                s = score_no(h, a)
                dve.wait_ge(score_done, s + 1)
                if s > 0:
                    dve.wait_ge(score_read, s)
                if a == 0 and h > 0:
                    dve.wait_ge(o_done, h)
                mk = masks[:, 64 * a:64 * a + (64 if a < len(LEVELS) else 128)]
                if a < len(LEVELS):
                    m = LEVELS[a]
                    at_ = attn[:, :, :].rearrange("p t (n s m) -> p t n s m", s=2, m=m)[:, :, :, 1, :]
                    mk = mk.rearrange("p (a n m) -> p a n m", a=1, m=m).to_broadcast([128, TT, 64 // m, m])
                    sc = score_bank[s % 2][:, 0:T // 2].rearrange("p (t n m) -> p t n m", t=TT, m=m)
                else:
                    at_ = attn[:, :, :]
                    mk = mk.rearrange("p (a n) -> p a n", a=1).to_broadcast([128, TT, 128])
                    sc = score_bank[s % 2][:, :].rearrange("p (t s) -> p t s", t=TT)
                V_.copy_predicated(at_, mk, sc).then_inc(score_read, 1)

            def step(kind, h, a):
                if kind == "A":
                    dve.wait_ge(lf_ready, h + 1)
                    link(V_.tensor_tensor_scan(b[:, :], restart[:, :], lf, 0.0, MULT, ADD))
                if kind == "L":
                    if a == 0:
                        dve.wait_ge(k_ready, h + 1)
                        dve.wait_ge(silu_done, SN["q", h] + 1)
                    differences(h, 2 * a)
                    differences(h, 2 * a + 1)
                    if a > 0:
                        take_scores(h, 2 * a - 2)
                        take_scores(h, 2 * a - 1)
                    factors(h, 2 * a)
                    factors(h, 2 * a + 1)
                if kind == "K":
                    b3 = b[:, :].rearrange("p (c t) -> p c t", t=CHUNK)
                    last = b3[:, :, CHUNK - 1:CHUNK].to_broadcast([128, NCH, CHUNK])
                    V_.tensor_tensor(kd[:, :].rearrange("p (c t) -> p c t", t=CHUNK), last, b3, SUB)\
                        .then_inc(diff_ready, 1)
                    take_scores(h, 4)
                    take_scores(h, 5)
                    dve.wait_ge(exp_ready, EXPS * h + DIFFS)
                    V_.tensor_tensor(kd[:, :], kd[:, :], fb[:, h % 2, :], MULT).then_inc(kd_ready, 1)
                if kind == "Q":
                    take_scores(h, 6)
                    dve.wait_ge(exp_ready, EXPS * (h + 1))
                    V_.tensor_tensor(qb[:, h % 2, :], qb[:, h % 2, :], eb[:, :], MULT).then_inc(qd_ready, 1)
                    dve.wait_ge(n_done, N["Q", h] + 1)
                    V_.tensor_copy(kdT[:, :, :], n_bank[:, :].rearrange("p (t k) -> p t k", t=TT))\
                        .then_inc(kdT_ready, 1)
                if kind == "S":
                    dve.wait_ge(n_done, N["S", h] + 1)
                    for c in range(NCH - 1):
                        u = (n_bank, o_bank)[c % 2][:, 128 * (c // 2):128 * (c // 2 + 1)]
                        if c == 0:
                            ins = V_.tensor_copy(S[:, 0, :], u)
                        else:
                            ins = V_.scalar_tensor_tensor(out=S[:, c, :], in0=S[:, c - 1, :],
                                                          scalar=eb[:, CHUNK * (c + 1) - 1:CHUNK * (c + 1)],
                                                          in1=u, op0=MULT, op1=ADD)
                        ins.then_inc(S_ready, 1)
                        dve.wait_ge(S_ready, (NCH - 1) * h + c + 1)
                if kind == "N":
                    dve.wait_ge(rms_ready, R["N", h] + 1)
                    V_.tensor_tensor(onrm, o_bank[:, :], osq[:, :], MULT).then_inc(o_read, 1)
                    dve.wait_ge(o_read, h + 1)
                    dve.wait_ge(silu_done, SN["g", h] + 1)
                    V_.scalar_tensor_tensor(out=onrm, in0=onrm, scalar=pcol("hgn", 0),
                                            in1=gb[:, h % 2, :], op0=MULT, op1=MULT).then_inc(cat_new, 1)
                    dve.wait_ge(cat_hi, h + 1)
                    V_.tensor_tensor(cat_l[:, h, :], onrm, cat_h[:, h, :].bitcast(f32), SUB)\
                        .then_inc(cat_lo, 1)

            for at, (kind, c) in enumerate(MIX_SLOTS):
                g = SLOT_GROUP[at]
                src = bank[g % 4][:, :]
                if kind in "qfg":
                    dst = {"q": qb, "f": fb, "g": gb}[kind][:, c % 2, :]
                    dve.wait_ge(unit_used, U_MIX + at + 1)
                    if kind == "q" and c >= 2:
                        dve.wait_ge(o_done, c - 1)
                    if kind == "f":
                        V_.tensor_tensor(dst, src, rstd[:, :], MULT).then_inc(group_read, 1)
                    else:
                        V_.scalar_tensor_tensor(out=dst, in0=src, scalar=0.5, in1=rstd[:, :], op0=MULT, op1=MULT)\
                            .then_inc(group_read, 1)
                        dve.wait_ge(act_out, FN[kind, c] + 1)
                        V_.scalar_tensor_tensor(out=dst, in0=half_tanh, scalar=1.0, in1=dst, op0=ADD, op1=MULT)\
                            .then_inc(silu_done, 1)
                elif kind in "BC":
                    dst = convB if kind == "B" else convC
                    dve.wait_ge(unit_used, U_MIX + at + 1)
                    V_.tensor_tensor(dst[:, :], src, rstd[:, :], MULT).then_inc(group_read, 1)
                elif kind == "u":
                    dve.wait_ge(unit_used, U_MIX + at + 1)
                    V_.tensor_tensor(convU[:, 2:], src, rstd[:, :], MULT).then_inc(group_read, 1)
                elif c == 0:
                    dve.wait_ge(rms_ready, R["mixcol"] + 1)
                    clear()
                elif c == 3:
                    dve.wait_ge(unit_used, U_MIX + at + 1)
                    for t in range(TT):
                        V_.tensor_scalar(V[:, t, :], bank[(G_V + t) % 4][:, :], cols[:, t:t + 1], None, MULT)\
                            .then_inc(group_read, 1)
                for st in STEPS[at]:
                    step(*st)
                if kind == "u":
                    dve.wait_ge(group_read, g + 5)
                    link(V_.tensor_tensor(convU[:, 2:], convU[:, 2:], convC[:, :], MULT))
                    w = [pcol("convw", CC * k + c) for k in range(3)]
                    link(V_.tensor_scalar(convV, convU[:, 2:], w[2], None, MULT))
                    link(V_.scalar_tensor_tensor(out=convV, in0=convU[:, 1:1 + T], scalar=w[1],
                                                 in1=convV, op0=MULT, op1=ADD))
                    link(V_.scalar_tensor_tensor(out=convV, in0=convU[:, 0:T], scalar=w[0],
                                                 in1=convV, op0=MULT, op1=ADD))
                    V_.tensor_tensor(convO[:, c, :], convV, convB[:, :], MULT).then_inc(conv_new, 1)
                    add_squares(Q_CONV + c)
            dve.wait_ge(rms_ready, R["conv"] + 1)
            for c in range(CC + 1):
                if c < CC:
                    V_.scalar_tensor_tensor(out=convO[:, c, :], in0=convO[:, c, :], scalar=pcol("convn", c),
                                            in1=osq[:, :], op0=MULT, op1=MULT).then_inc(cat_new, 1)
                if c > 0:
                    dve.wait_ge(cat_hi, HEADS + c)
                    V_.tensor_tensor(cat_l[:, HEADS + c - 1, :], convO[:, c - 1, :],
                                     cat_h[:, HEADS + c - 1, :].bitcast(f32), SUB).then_inc(cat_lo, 1)
            clear()
            V_.memset(rstd[:, M:2 * M], 0.0).then_inc(msq_added, 1)
            for m in range(KC):
                if m == 4:
                    dve.wait_ge(rms_ready, R["mem"] + 1)
                    for k in range(KC):
                        V_.scalar_tensor_tensor(out=memf[:, k, :], in0=memf[:, k, :], scalar=pcol("mem", k),
                                                in1=rstd[:, 0:M], op0=MULT, op1=MULT).then_inc(mem_norm, 1)
                    for k in range(KC):
                        dve.wait_ge(mem_hi, k + 1)
                        V_.tensor_tensor(ml[:, k, :], memf[:, k, :], mh[:, k, :].bitcast(f32), SUB)\
                            .then_inc(mem_lo, 1)
                update_x(m, G_WOUT, U_WOUT, 1.0)
                if m == 1:
                    for k in range(KC):
                        dve.wait_ge(msq_ready, k + 1)
                        dve.wait_ge(msq_added, k + 1)
                        V_.tensor_tensor(rstd[:, M:2 * M], rstd[:, M:2 * M], ubuf[:, k % 2, 0:M], ADD)\
                            .then_inc(msq_added, 1)
                chunk_lo(2, m, Q_X2)
            for g in range(KC):
                dve.wait_ge(kv_hi, g + 1)
                V_.tensor_tensor(kTl[:, g, :], bank[(G_KT + g) % 4][:, 0:M], kTh[:, g, :].bitcast(f32), SUB)\
                    .then_inc(group_read, 1)
            norm_of("xa")
            for kind, i in XA_ORDER + [("T", 3), ("O", 3)]:
                if kind == "q":
                    g = XG["q", i]
                    dve.wait_ge(unit_used, XU["q", i] + 1)
                    V_.tensor_tensor(gbuf[:, i % 2, :], bank[g % 4][:, :], rstd[:, :], MULT).then_inc(group_read, 1)
                    dve.wait_ge(q_hi, i + 1)
                    slot = (i // 2) % 2
                    V_.tensor_tensor(qhl[:, slot, 1, i % 2, :], gbuf[:, i % 2, :], qhl[:, slot, 0, i % 2, :].bitcast(f32),
                                     SUB).then_inc(q_lo, 1)
                if kind == "vx":
                    for t in range(2):
                        cs = slice(512 * i, 512 * i + 512)
                        dve.wait_ge(kv_hi, KC + 2 * i + t + 1)
                        V_.tensor_tensor(vxl[:, t, cs], bank[(XG["vx", i] + t) % 4][:, :],
                                         vxh[:, t, cs].bitcast(f32), SUB).then_inc(group_read, 1)
                if kind == "S":
                    dve.wait_ge(xs_done, i + 1)
                    for n in range(2):
                        link(V_.reduce_max(smax[:, 2 * n:2 * n + 2],
                                           score_bank[n][:, :].rearrange("p (t m) -> p t m", m=M), AX.X))
                    V_.tensor_scalar(smax[:, :], smax[:, :], -1.0 / 16, None, MULT).then_inc(xmax_ready, 1)
                    dve.wait_ge(p_exp, TT * (i + 1))
                    link(V_.reciprocal(ssum[:, :], ssum[:, :]))
                    V_.tensor_tensor(P[:, :, :], P[:, :, :],
                                     ssum[:, :].rearrange("p (t a) -> p t a", a=1).to_broadcast([128, TT, M]),
                                     MULT).then_inc(p_ready, 1)
                if kind == "T":
                    for t, bk in enumerate((o_bank, n_bank)):
                        dve.wait_ge(pt_hi, 2 * i + t + 1)
                        V_.tensor_tensor(pTl[:, t, :], bk[:, :], pTh[:, t, :].bitcast(f32), SUB)\
                            .then_inc(pt_lo, 1)
                if kind == "O":
                    for d, bk in enumerate((o_bank, n_bank)):
                        dve.wait_ge(cat_hi, KC + 2 * i + d + 1)
                        V_.tensor_tensor(cat_l[:, 2 * i + d, :], bk[:, :], cat_h[:, 2 * i + d, :].bitcast(f32), SUB)\
                            .then_inc(cat_lo, 1)
            for m in range(KC):
                update_x(m, G_WO, U_WO, 1.0)
                chunk_lo(3, m, Q_X3)
            ffn("ffn2", 1)
            for h in range(2):
                if h == 0:
                    dve.wait_ge(half_done, 1)
                else:
                    dve.wait_ge(unit_used, NU)
                xs = x[:, KC - 1, HALVES[h]]
                V_.scalar_tensor_tensor(out=xs, in0=bank[(G_DOWN2 + KC - 1 + h) % 4][:, HALVES[h]], scalar=0.5, in1=xs,
                                        op0=MULT, op1=ADD).then_inc(x_half, 1)
                dve.wait_ge(rms_ready, R["final"] + h + 1)
                for m in range(KC):
                    xs = x[:, m, HALVES[h]]
                    V_.scalar_tensor_tensor(out=xs, in0=xs, scalar=pcol("final", m), in1=rstd[:, HALVES[h]],
                                            op0=MULT, op1=MULT).then_inc(cat_new, 1)

        @block.tensor
        def _(pe):
            def product(out_, a, b_, first, last):
                nc.tensor.matmul(out_, a[0], b_[0], start=first, stop=False)
                nc.tensor.matmul(out_, a[0], b_[1], start=False, stop=False)
                return nc.tensor.matmul(out_, a[1], b_[0], start=False, stop=last)

            def wpair(slot, lo, hi_):
                return wh[:, slot, lo:hi_], wl[:, slot, lo:hi_]

            def group(u, g, off_u=None, off_g=None, x_phase=None, src=(xh, xl), cols_=T, ready=None):
                ou = 0 if off_u is None else off_u
                og = 0 if off_g is None else off_g
                slot = u % SLOTS
                pe.wait_ge(lo_ready, ou + (u + 1))
                pe.wait_ge(group_read, og + (g + 1))
                for k in range(KC):
                    if x_phase is not None:
                        pe.wait_ge(x_lo, KC * x_phase + k + 1)
                    if ready is not None:
                        pe.wait_ge(ready[0], ready[1] + k + 1)
                    last = product(bank[g % 4][:, 0:cols_], wpair(slot, 128 * k, 128 * k + 128),
                                   (src[0][:, k, :], src[1][:, k, :]), k == 0, k == KC - 1)
                last.then_inc(unit_used, 1)

            def n_wait(name):
                if N[name] == 0:
                    return
                prev = n_uses[N[name] - 1]
                if prev[0] == "Q":
                    pe.wait_ge(kdT_ready, prev[1] + 1)
                elif prev[0] == "S":
                    pe.wait_ge(S_ready, (NCH - 1) * (prev[1] + 1))
                elif prev[0] == "T":
                    pe.wait_ge(pt_lo, 2 * prev[1] + 2)
                elif prev[0] == "O":
                    pe.wait_ge(cat_lo, KC + 2 * prev[1] + 2)
                else:
                    pe.wait_ge(rms_ready, R[prev] + 1)

            def sum_squares(name, added):
                pe.wait_ge(sq_added, added)
                n_wait(name)
                nc.tensor.matmul(n_bank[:, :], ones[:, :], acc[:, :], start=True, stop=True)\
                    .then_inc(n_done, 1)

            def ffn(which, norm, qn):
                u0, g0, hb = (U_FFN1, G_UP1, 0) if which == 0 else (U_FFN2, G_UP2, FC)
                ph = 0 if which == 0 else 3
                if which == 0:
                    pe.wait_ge(group_read, 1)
                    pe.wait_ge(hi_ready, 1)
                    for k in range(KC):
                        pe.wait_ge(x_hi, k + 1)
                        nc.tensor.matmul(bank[0][:, :], wh[:, 0, 128 * k:128 * k + 128], xh[:, k, :],
                                         start=(k == 0), stop=False)
                    pe.wait_ge(lo_ready, 1)
                    for k in range(KC):
                        pe.wait_ge(x_lo, k + 1)
                        nc.tensor.matmul(bank[0][:, :], wh[:, 0, 128 * k:128 * k + 128], xl[:, k, :],
                                         start=False, stop=False)
                        last = nc.tensor.matmul(bank[0][:, :], wl[:, 0, 128 * k:128 * k + 128], xh[:, k, :],
                                                start=False, stop=(k == KC - 1))
                    last.then_inc(unit_used, 1)
                    group(u0 + 1, g0 + 1)
                    sum_squares(norm, qn + KC)
                else:
                    group(u0, g0, x_phase=ph)
                    sum_squares(norm, qn + KC)
                    group(u0 + 1, g0 + 1)
                for c in range(2, 4):
                    group(u0 + c, g0 + c)
                with pe.Fori(1, FC // 2) as i:
                    for c in range(4):
                        group(u0 + c, g0 + c, i * 4, i * 4)
                ud, gd, nd = u0 + N_UP, g0 + N_UP, len(DOWN_SPLIT)

                def down(m, i=None):
                    pe.wait_ge(group_read, (0 if i is None else i * 4) + (gd + m + 1))
                    j = 0
                    for c, n in enumerate(DOWN_SPLIT):
                        u = ud + m * nd + c
                        pe.wait_ge(lo_ready, (0 if i is None else i * (4 * nd)) + (u + 1))
                        for k in range(n):
                            if m == 0:
                                pe.wait_ge(hid_lo, hb + j + 1)
                            hs = slice(j * T, (j + 1) * T)
                            last = product(bank[(gd + m) % 4][:, :], wpair(u % SLOTS, 128 * k, 128 * k + 128),
                                           (hid_h[:, hs], hid_l[:, hs]), j == 0, j == FC - 1)
                            j += 1
                        last.then_inc(unit_used, 1)

                if which == 0:
                    with pe.Fori(0, KC // 4) as i:
                        for m in range(4):
                            down(m, i)
                    return
                for m in range(KC - 1):
                    down(m)
                for h in range(2):
                    pe.wait_ge(group_read, gd + KC + h)
                    j = 0
                    for c, n in enumerate(DOWN_SPLIT):
                        u = ud + (KC - 1) * nd + c
                        if h == 0:
                            pe.wait_ge(lo_ready, u + 1)
                        for k in range(n):
                            hs = slice(j * T + T // 2 * h, j * T + T // 2 * (h + 1))
                            last = product(bank[(gd + KC - 1 + h) % 4][:, HALVES[h]], wpair(u % SLOTS, 128 * k, 128 * k + 128),
                                           (hid_h[:, hs], hid_l[:, hs]), j == 0, j == FC - 1)
                            j += 1
                            if h == 1 and j == 6:
                                final_sum(0)
                        if h == 1:
                            last.then_inc(unit_used, 1)
                    if h == 0:
                        last.then_inc(half_done, 1)

            def final_sum(h):
                if h == 0:
                    pe.wait_ge(sq_added, Q_X4 + KC - 1)
                    n_wait("final")
                pe.wait_ge(sq_half, h + 1)
                bk = (n_bank, o_bank)[h][:, HALVES[h]]
                nc.tensor.matmul(bk, ones[:, :], acc[:, HALVES[h]], start=True, stop=False)
                nc.tensor.matmul(bk, ones[:, :], sq[:, 1, HALVES[h]], start=False, stop=True).then_inc(n_done, 1)

            pe.wait_ge(consts_ready, 1)
            ffn(0, "ffn1", Q_X0)

            def step(kind, h, a):
                if kind in ("L", "K", "Q"):
                    first = {"L": 2 * a - 2, "K": 4, "Q": 6}[kind]
                    for l in range(first, min(first + 2, NL)) if first >= 0 else ():
                        s = score_no(h, l)
                        if l < len(LEVELS):
                            pe.wait_ge(score_in, len(LEVELS) * h + l + 1)
                            lhs = X[:, l % 2, :]
                            rhs = lhs.rearrange("p (t n s m) -> p t n s m", t=TT, s=2, m=LEVELS[l])[:, :, :, 1, :]
                            width = 64
                        else:
                            lhs = fb[:, h % 2, :]
                            rhs = qb[:, h % 2, :].rearrange("p (t s) -> p t s", t=TT)
                            width = 128
                        if s >= 2:
                            pe.wait_ge(score_read, s - 1)
                        for t in range(TT):
                            last = nc.tensor.matmul(score_bank[s % 2][:, width * t:width * (t + 1)],
                                                    lhs[:, 128 * t:128 * t + 128], rhs[:, t], start=True, stop=True)
                        last.then_inc(score_done, 1)
                if kind == "Q":
                    pe.wait_ge(kd_ready, h + 1)
                    if h == 0:
                        pe.wait_ge(ident_loaded, 16)
                    n_wait(("Q", h))
                    for t in range(TT):
                        ts = slice(128 * t, 128 * t + 128)
                        last = nc.tensor.transpose(n_bank[:, ts], kd[:, ts], ident[:, :])
                    last.then_inc(n_done, 1)
                if kind == "S":
                    pe.wait_ge(kdT_ready, h + 1)
                    pe.wait_ge(group_read, G_V + TT + 4)
                    n_wait(("S", h))
                    if h > 0:
                        pe.wait_ge(o_read, h)
                    for half, bk in enumerate((n_bank, o_bank)):
                        for c in range(half, NCH - 1, 2):
                            rows = slice(64 * half, 64 * half + 64)
                            last = nc.tensor.matmul(bk[:, 128 * (c // 2):128 * (c // 2 + 1)],
                                                    kdT[rows, c // 2, :], V[rows, c // 2, 128 * h:128 * h + 128],
                                                    start=True, stop=True)
                    last.then_inc(n_done, 1)
                if kind == "O":
                    pe.wait_ge(S_ready, (NCH - 1) * (h + 1))
                    pe.wait_ge(score_read, NL * (h + 1))
                    for t in range(TT):
                        ts = slice(128 * t, 128 * t + 128)
                        nc.tensor.matmul(o_bank[:, ts], V[:, t, 128 * h:128 * h + 128], attn[:, t, :],
                                         start=(t == 0), stop=False, skip_group_check=True)
                    pe.wait_ge(qd_ready, h + 1)
                    for c in range(1, NCH):
                        cs = slice(CHUNK * c, CHUNK * c + CHUNK)
                        last = nc.tensor.matmul(o_bank[:, cs], S[:, c - 1, :], qb[:, h % 2, cs],
                                                start=False, stop=(c == NCH - 1), skip_group_check=True)
                    last.then_inc(o_done, 1)
                if kind == "N":
                    pe.wait_ge(osq_ready, h + 1)
                    n_wait(("N", h))
                    nc.tensor.matmul(n_bank[:, :], ones[:, :], osq[:, :], start=True, stop=True).then_inc(n_done, 1)

            for at, (kind, c) in enumerate(MIX_SLOTS):
                u = U_MIX + at
                if kind == "v":
                    pe.wait_ge(lo_ready, u + 1)
                    for t in range(TT):
                        g = G_V + t
                        if c == 0:
                            pe.wait_ge(group_read, g + 1)
                        for kk in range(2):
                            k = 2 * c + kk
                            ts = slice(128 * t, 128 * t + 128)
                            last = product(bank[g % 4][:, :], (xh[:, k, ts], xl[:, k, ts]),
                                           wpair(u % SLOTS, 512 * kk, 512 * kk + 512), k == 0, k == KC - 1)
                    last.then_inc(unit_used, 1)
                else:
                    group(u, SLOT_GROUP[at], x_phase=1 if at == 0 else None)
                if at == 0:
                    sum_squares("mix", Q_X1 + KC)
                if at == 1:
                    n_wait("mixcol")
                    for t in range(TT):
                        last = nc.tensor.matmul(n_bank[:, t:t + 1], acc[:, 128 * t:128 * t + 128], ones[:, 0:1],
                                                start=True, stop=True)
                    last.then_inc(n_done, 1)
                for st in STEPS[at]:
                    step(*st)
            def together(u0, g0, at_k, ready):

                def part(c, k):
                    return product(bank[(g0 + c) % 4][:, :], wpair((u0 + c) % SLOTS, 128 * k, 128 * k + 128),
                                   (cat_h[:, k, :], cat_l[:, k, :]), k == 0, k == KC - 1)

                pe.wait_ge(cat_lo, ready + 2)
                for c in range(4):
                    pe.wait_ge(lo_ready, u0 + c + 1)
                    pe.wait_ge(group_read, g0 + c + 1)
                    part(c, 0)
                    part(c, 1)
                for k in range(2, KC - 2):
                    pe.wait_ge(cat_lo, ready + k + 1)
                    for c in range(4):
                        part(c, k)
                    if k in at_k:
                        at_k[k]()
                pe.wait_ge(cat_lo, ready + KC)
                for c in range(4):
                    part(c, KC - 2)
                    part(c, KC - 1).then_inc(unit_used, 1)

            together(U_WOUT, G_WOUT, {2: lambda: sum_squares("conv", Q_CONV + CC)}, 0)
            for m in range(4, KC):
                group(U_WOUT + m, G_WOUT + m, src=(cat_h, cat_l))
                if m == 4:
                    pe.wait_ge(msq_added, KC + 1)
                    n_wait("mem")
                    nc.tensor.matmul(n_bank[:, 0:M], ones[:, :], rstd[:, M:2 * M], start=True, stop=True)\
                        .then_inc(n_done, 1)
            for g in range(KC):
                group(U_KT + g, G_KT + g, src=(mh, ml), cols_=M, ready=(mem_lo, 0) if g == 0 else None)
                if g == 3:
                    sum_squares("xa", Q_X2 + KC)
            def xa_step(kind, i):
                if kind == "q":
                    group(XU["q", i], XG["q", i], x_phase=2 if i == 0 else None)
                if kind == "vx":
                    for k2 in range(4):
                        u = XU["vx", i] + k2
                        pe.wait_ge(lo_ready, u + 1)
                        for t in range(2):
                            g = XG["vx", i] + t
                            if k2 == 0:
                                pe.wait_ge(group_read, g + 1)
                            for kk in range(2):
                                k = 2 * k2 + kk
                                ts = slice(128 * t, 128 * t + 128)
                                last = product(bank[g % 4][:, :], (mh[:, k, ts], ml[:, k, ts]),
                                               wpair(u % SLOTS, 512 * kk, 512 * kk + 512), k == 0, k == KC - 1)
                        last.then_inc(unit_used, 1)
                if kind == "S":
                    pe.wait_ge(q_lo, 2 * i + 2)
                    if i == 0:
                        pe.wait_ge(group_read, G_KT + KC + 4)
                    else:
                        pe.wait_ge(p_exp, TT * i)
                    for t in range(TT):
                        ts = slice(128 * t, 128 * t + 128)
                        for d in range(2):
                            last = product(score_bank[t // 2][:, (t % 2) * M:(t % 2 + 1) * M],
                                           (qhl[:, i % 2, 0, d, ts], qhl[:, i % 2, 1, d, ts]),
                                           (kTh[:, 2 * i + d, :], kTl[:, 2 * i + d, :]), d == 0, d == 1)
                    last.then_inc(xs_done, 1)
                if kind == "T":
                    pe.wait_ge(p_ready, i + 1)
                    n_wait(("T", i))
                    for t2, bk in enumerate((o_bank, n_bank)):
                        for t in range(TT):
                            last = nc.tensor.transpose(bk[:, 128 * t:128 * t + 128],
                                                       P[:, t, 128 * t2:128 * t2 + 128], ident[:, :])
                    last.then_inc(n_done, 1)
                if kind == "O":
                    n_wait(("O", i))
                    pe.wait_ge(group_read, XG["vx", i // 2] + 2 + 4)
                    for d, bk in enumerate((o_bank, n_bank)):
                        ds_ = slice(256 * i + 128 * d, 256 * i + 128 * d + 128)
                        for t in range(2):
                            last = product(bk[:, :], (vxh[:, t, ds_], vxl[:, t, ds_]),
                                           (pTh[:, t, :], pTl[:, t, :]), t == 0, t == 1)
                    last.then_inc(n_done, 1)

            for kind, i in XA_ORDER:
                xa_step(kind, i)
            together(U_WO, G_WO, {2: lambda: xa_step("T", 3), 4: lambda: xa_step("O", 3)}, KC)
            for m in range(4, KC):
                group(U_WO + m, G_WO + m, src=(cat_h, cat_l))
            ffn(1, "ffn2", Q_X3)
            final_sum(1)


def _pack_weights(w):
    import numpy as np

    units = np.zeros((NU, 128, UNIT), np.float32)

    def k_major(mat):
        return mat.reshape(-1, 128, mat.shape[1]).transpose(1, 0, 2).reshape(128, -1)

    def cols128(mat, c):
        return k_major(mat[:, 128 * c:128 * c + 128])

    for u0, gu, down in ((U_FFN1, w["ffn1_w_gu"][0], w["ffn1_w_down"][0]), (U_FFN2, w["ffn2_w_gu"][0], w["ffn2_w_down"][0])):
        for j in range(FC):
            units[u0 + 2 * j] = cols128(gu, j)
            units[u0 + 2 * j + 1] = cols128(gu, FC + j)
        u = u0 + N_UP
        for m in range(KC):
            whole, at = cols128(down, m), 0
            for n in DOWN_SPLIT:
                units[u, :, :128 * n] = whole[:, 128 * at:128 * (at + n)]
                at += n
                u += 1
    w_in = w["w_in"][0]
    first = {"q": 0, "f": 4, "g": 12, "B": 16, "C": 20, "u": 24}
    for at, (kind, c) in enumerate(MIX_SLOTS):
        if kind == "v":
            units[U_MIX + at] = k_major(w_in[256 * c:256 * c + 256, 1024:1536])
        else:
            units[U_MIX + at] = cols128(w_in, first[kind] + c)
    for m in range(KC):
        units[U_WOUT + m] = cols128(w["w_out"][0], m)
        units[U_KT + m] = cols128(w["xa_wkv"][0], m)
        units[XU["q", m]] = cols128(w["xa_wq"][0], m)
        units[U_WO + m] = cols128(w["xa_wo"][0], m)
    for half in range(2):
        for k2 in range(4):
            units[XU["vx", half] + k2] = k_major(
                w["xa_wkv"][0][256 * k2:256 * k2 + 256, D + 512 * half:D + 512 * half + 512])
    return units


def _level_masks():
    import numpy as np

    s, t = np.arange(128)[:, None], np.arange(128)[None, :]
    masks = [(s // (2 * m) == t // (2 * m)) & (s % (2 * m) < m) & (t % (2 * m) >= m) for m in LEVELS]
    masks = [mask[:, np.arange(128) % (2 * m) >= m] for mask, m in zip(masks, LEVELS)]
    return np.concatenate(masks + [s == t], 1).astype(np.float32)


def kernel(**inputs):
    import numpy as np
    import concourse.bacc as bacc
    from concourse.bass_utils import run_bass_kernel_spmd

    w = {n: np.asarray(a) for n, a in inputs.items()}
    x_t = np.ascontiguousarray(w["x"][0].T).reshape(KC, 128, T)
    mem_t = np.ascontiguousarray(w["mem"][0].T.reshape(KC, 128, M).transpose(1, 0, 2))

    def column(v):
        return v.reshape(-1, 128).T

    params = np.ascontiguousarray(np.concatenate([
        column(w["ffn1_norm"][0]), column(w["mix_norm"][0]), column(w["xa_norm"][0]), column(w["ffn2_norm"][0]),
        column(w["final_norm"]), column(w["mem_norm"][0]), column(w["hg_norm"][0]), column(w["conv_norm"][0]),
        column(w["conv_w"][0].reshape(-1)), column(w["lb_logits"].reshape(-1))], axis=1))
    arrays = {"w_all": _pack_weights(w), "x_t": x_t, "mem_t": mem_t, "params": params,
              "masks_d": _level_masks(), "ident_d": np.eye(128, dtype=np.float32)}
    nc = bacc.Bacc("TRN2", target_bir_lowering=False, num_devices=1)
    args = [nc.dram_tensor(n, a.shape, mybir.dt.from_np(a.dtype), kind="ExternalInput").ap() for n, a in arrays.items()]
    out = nc.dram_tensor("out_t", (KC, 128, T), mybir.dt.float32, kind="ExternalOutput").ap()
    block_kernel(nc, *args, out)
    r = run_bass_kernel_spmd(nc, [arrays], core_ids=[0])
    got = r.results[0]["out_t"]
    return np.ascontiguousarray(got.reshape(D, T).T)[None]
```
